# Optimizing a Trainium2 kernel written in Bass

```python
import jax, jax.numpy as jnp
from jax import lax
import numpy as np

D_MODEL = 1024
BATCH = 1
SEQ = 256
DEPTH = 2

EXPAND = 2
D_INNER = EXPAND * D_MODEL
POOL_WINDOWS = (2, 4, 8, 16)
N_POOL_GROUPS = len(POOL_WINDOWS)
POOL_GROUP_DIM = D_INNER // N_POOL_GROUPS
HEAD_DIM = 128
N_HEADS = D_INNER // HEAD_DIM
MOBA_BLOCK = 256
MOBA_TOPK = 3
Q_CHUNK = 16
ROPE_THETA = 10000.0
EPS = 1e-6
N_MIXERS = 2

kernel_name = "hybrid_pool_moba_gated"

def rms_norm(x, g):
    xf = x.astype(jnp.float32)
    y = xf * lax.rsqrt(jnp.mean(xf * xf, axis=-1, keepdims=True) + EPS)
    return (y * g.astype(jnp.float32)).astype(x.dtype)

def rope(x):
    S = x.shape[2]
    inv = ROPE_THETA ** (-jnp.arange(0, HEAD_DIM, 2, dtype=jnp.float32) / HEAD_DIM)
    ang = jnp.arange(S, dtype=jnp.float32)[:, None] * inv[None, :]
    cos, sin = jnp.cos(ang), jnp.sin(ang)
    xf = x.astype(jnp.float32)
    x1, x2 = xf[..., : HEAD_DIM // 2], xf[..., HEAD_DIM // 2:]
    out = jnp.concatenate([x1 * cos - x2 * sin, x2 * cos + x1 * sin], axis=-1)
    return out.astype(x.dtype)

def pool_mixer(u, w_pool, pool_scale):
    B, S, _ = u.shape
    uf = u.astype(jnp.float32).reshape(B, S, N_POOL_GROUPS, POOL_GROUP_DIM)
    cs = jnp.cumsum(uf, axis=1)
    pos = jnp.arange(1, S + 1, dtype=jnp.float32)
    outs = []
    for g, w in enumerate(POOL_WINDOWS):
        cg = cs[:, :, g]
        lag = jnp.pad(cg, ((0, 0), (w, 0), (0, 0)))[:, :S]
        cnt = jnp.minimum(pos, float(w))[None, :, None]
        outs.append((cg - lag) / cnt - uf[:, :, g])
    pooled = jnp.stack(outs, axis=2).astype(u.dtype)
    mixed = jnp.einsum('bsgc,gcd->bsgd', pooled, w_pool).reshape(B, S, D_INNER)
    return mixed * pool_scale

def pool_layer(x, norm_g, w_in, w_pool, pool_scale, w_out):
    h = rms_norm(x, norm_g)
    u, z = jnp.split(h @ w_in, 2, axis=-1)
    y = pool_mixer(u, w_pool, pool_scale) * jax.nn.silu(z)
    return x + y @ w_out

def moba_attention(q, k, v):
    B, H, S, dh = q.shape
    nb = -(-S // MOBA_BLOCK)
    pad = nb * MOBA_BLOCK - S
    kp = jnp.pad(k, ((0, 0), (0, 0), (0, pad), (0, 0)))
    vp = jnp.pad(v, ((0, 0), (0, 0), (0, pad), (0, 0)))
    kb = kp.reshape(B, H, nb, MOBA_BLOCK, dh)
    vb = vp.reshape(B, H, nb, MOBA_BLOCK, dh)
    k_mean = jnp.mean(kb.astype(jnp.float32), axis=3)

    q_blk = jnp.arange(S) // MOBA_BLOCK
    gate = jnp.einsum('bhsd,bhnd->bhsn', q.astype(jnp.float32), k_mean)
    past = jnp.arange(nb)[None, :] < q_blk[:, None]
    gate = jnp.where(past, gate, -jnp.inf)
    n_sel = min(MOBA_TOPK, nb)
    _, sel = lax.top_k(gate, n_sel)
    sel_valid = sel < q_blk[:, None]

    nc = S // Q_CHUNK

    def to_chunks(t):
        return jnp.moveaxis(t.reshape(B, H, nc, Q_CHUNK, *t.shape[3:]), 2, 0)

    scale = HEAD_DIM ** -0.5
    gather = jax.vmap(jax.vmap(lambda blocks, idx: blocks[idx]))

    def chunk_fn(args):
        c, qc, selc, validc = args
        start = c * Q_CHUNK
        own = start // MOBA_BLOCK
        k_own = lax.dynamic_slice_in_dim(kp, own * MOBA_BLOCK, MOBA_BLOCK, axis=2)
        v_own = lax.dynamic_slice_in_dim(vp, own * MOBA_BLOCK, MOBA_BLOCK, axis=2)
        q_pos = start + jnp.arange(Q_CHUNK)
        k_pos = own * MOBA_BLOCK + jnp.arange(MOBA_BLOCK)
        s_own = jnp.einsum('bhqd,bhkd->bhqk', qc, k_own).astype(jnp.float32) * scale
        s_own = jnp.where(k_pos[None, :] <= q_pos[:, None], s_own, -jnp.inf)
        k_sel = gather(kb, selc)
        v_sel = gather(vb, selc)
        s_sel = jnp.einsum('bhqd,bhqnkd->bhqnk', qc, k_sel).astype(jnp.float32) * scale
        s_sel = jnp.where(validc[..., None], s_sel, -jnp.inf)
        s = jnp.concatenate([s_own, s_sel.reshape(B, H, Q_CHUNK, n_sel * MOBA_BLOCK)], axis=-1)
        p = jax.nn.softmax(s, axis=-1).astype(v.dtype)
        p_own = p[..., :MOBA_BLOCK]
        p_sel = p[..., MOBA_BLOCK:].reshape(B, H, Q_CHUNK, n_sel, MOBA_BLOCK)
        return (jnp.einsum('bhqk,bhkd->bhqd', p_own, v_own)
                + jnp.einsum('bhqnk,bhqnkd->bhqd', p_sel, v_sel))

    out = lax.map(chunk_fn, (jnp.arange(nc), to_chunks(q), to_chunks(sel), to_chunks(sel_valid)))
    return jnp.moveaxis(out, 0, 2).reshape(B, H, S, dh)

def moba_layer(x, norm_g, w_in, q_norm, k_norm, w_out):
    B, S, _ = x.shape
    h = rms_norm(x, norm_g)
    q, k, v, z = jnp.split(h @ w_in, 4, axis=-1)

    def heads(t):
        return t.reshape(B, S, N_HEADS, HEAD_DIM).transpose(0, 2, 1, 3)

    q = rope(rms_norm(heads(q), q_norm))
    k = rope(rms_norm(heads(k), k_norm))
    v = heads(v)
    o = moba_attention(q, k, v).transpose(0, 2, 1, 3).reshape(B, S, D_INNER)
    return x + (o * jax.nn.silu(z)) @ w_out

def setup_inputs(seed: int = 0) -> dict:
    key = jax.random.key(seed)
    ks = jax.random.split(key, 12)
    f32 = jnp.float32
    nrm = jax.random.normal
    x = nrm(ks[0], (BATCH, SEQ, D_MODEL), f32)
    norm0 = 1.0 + 0.02 * nrm(ks[1], (D_MODEL,), f32)
    w_in0 = nrm(ks[2], (D_MODEL, 2 * D_INNER), f32) * D_MODEL ** -0.5
    w_pool0 = nrm(ks[3], (N_POOL_GROUPS, POOL_GROUP_DIM, POOL_GROUP_DIM), f32) * POOL_GROUP_DIM ** -0.5
    pool_scale0 = 1.0 + 0.02 * nrm(ks[4], (D_INNER,), f32)
    w_out0 = nrm(ks[5], (D_INNER, D_MODEL), f32) * D_INNER ** -0.5
    norm1 = 1.0 + 0.02 * nrm(ks[6], (D_MODEL,), f32)
    w_in1 = nrm(ks[7], (D_MODEL, 4 * D_INNER), f32) * D_MODEL ** -0.5
    q_norm1 = 1.0 + 0.02 * nrm(ks[8], (HEAD_DIM,), f32)
    k_norm1 = 1.0 + 0.02 * nrm(ks[9], (HEAD_DIM,), f32)
    w_out1 = nrm(ks[10], (D_INNER, D_MODEL), f32) * D_INNER ** -0.5
    return {"x": x,
            "norm0": norm0, "w_in0": w_in0, "w_pool0": w_pool0,
            "pool_scale0": pool_scale0, "w_out0": w_out0,
            "norm1": norm1, "w_in1": w_in1, "q_norm1": q_norm1,
            "k_norm1": k_norm1, "w_out1": w_out1}

def reference(x, norm0, w_in0, w_pool0, pool_scale0, w_out0,
              norm1, w_in1, q_norm1, k_norm1, w_out1):
    layers = (
        (pool_layer, (norm0, w_in0, w_pool0, pool_scale0, w_out0)),
        (moba_layer, (norm1, w_in1, q_norm1, k_norm1, w_out1)),
    )
    for i in range(DEPTH):
        layer_fn, params = layers[i]
        x = layer_fn(x, *params)
    return x


_drawn_inputs = setup_inputs


def setup_inputs(seed=0):
    import zlib

    import numpy as np

    out = dict(_drawn_inputs(seed))
    spreads = {}
    factors = {'norm0': 3.919, 'pool_scale0': 6.169, 'norm1': 8.0, 'q_norm1': 8.0, 'k_norm1': 8.0}
    for name, (base, spread) in spreads.items():
        noise = np.random.default_rng([zlib.crc32(name.encode()), seed]).standard_normal(out[name].shape)
        drawn = base * np.exp(spread * noise) if base else spread * noise
        out[name] = __import__('jax').numpy.asarray(drawn.astype(out[name].dtype))
    for name, factor in factors.items():
        out[name] = (out[name] * factor).astype(out[name].dtype)
    return out
```

```python
from contextlib import ExitStack

import numpy as np

import concourse.bass as bass
from concourse import mybir

F32 = mybir.dt.float32
F32R = mybir.dt.float32r
BF16 = mybir.dt.bfloat16
ALU = mybir.AluOpType
ACT = mybir.ActivationFunctionType
AX_X = mybir.AxisListType.X

P = 128
SEQ = 256
D_MODEL = 1024
D_INNER = 2048
HEAD_DIM = 128
POOL_WINDOWS = (2, 4, 8, 16)
ROPE_THETA = 10000.0
EPS = 1e-6

TT = SEQ // P
KD = D_MODEL // P
KI = D_INNER // P
COLS = 512
GK = 4
GROUPS = D_INNER // COLS
HPG = COLS // HEAD_DIM
RING = 4
EDGE = max(POOL_WINDOWS)
BAND = P + EDGE
POOL_COLS = BAND + 2 * EDGE
MASKED = -1e30

N_POOL = 4 * GROUPS
N_OUT0 = N_POOL + GROUPS
N_L1 = N_OUT0 + 2 * (KI // GK)
N_OUT1 = N_L1 + 8 * GROUPS
N_END = N_OUT1 + 8
OUT1_ORDER = [(0, 0), (0, 1), (0, 2), (1, 0), (1, 1), (1, 2), (0, 3), (1, 3)]

C_COS = 0
C_SIN = C_COS + TT * HEAD_DIM
C_MASK = C_SIN + TT * HEAD_DIM
C_END = C_MASK + P


def constant_tables():
    s, t = np.arange(P)[:, None], np.arange(BAND)[None, :]
    pool = np.zeros((P, GROUPS, POOL_COLS), np.float32)
    for g, w in enumerate(POOL_WINDOWS):
        inside = ((t - s >= 0) & (t - s < w)).astype(np.float32)
        own = (t == s).astype(np.float32)
        pool[:, g, :BAND] = inside / np.float32(w) - own
        count = np.minimum(np.arange(EDGE) + 1, w).astype(np.float32)
        pool[:, g, BAND:BAND + EDGE] = inside[:, :EDGE] / count - own[:, :EDGE]
    inv = np.float32(ROPE_THETA) ** (-np.arange(0, HEAD_DIM, 2, dtype=np.float32) / np.float32(HEAD_DIM))
    ang = np.arange(SEQ, dtype=np.float32)[:, None] * inv[None, :].astype(np.float32)
    cos, sin = np.cos(ang), np.sin(ang)
    cos2 = np.concatenate([cos, cos], 1).reshape(TT, P, HEAD_DIM).transpose(1, 0, 2)
    sin2 = np.concatenate([-sin, sin], 1).reshape(TT, P, HEAD_DIM).transpose(1, 0, 2)
    mask = np.where(np.arange(P)[None, :] <= np.arange(P)[:, None], 0.0, MASKED)
    parts = [cos2, sin2, mask]
    table = np.concatenate([a.reshape(P, -1) for a in parts], 1).astype(np.float32)
    assert table.shape[1] == C_END
    return table, pool.reshape(P, -1), np.eye(P, dtype=np.float32)


class Chain:

    def __init__(self, eng, sem):
        self.eng, self.sem, self.base, self.made = eng, sem, 0, 0

    def mark(self, ins):
        ins.then_inc(self.sem, 1)
        self.made += 1
        return self.base + self.made

    def wait(self, value):
        self.eng.wait_ge(self.sem, value)

    def done(self, ins):
        self.wait(self.mark(ins))

    def rebase(self, base):
        self.base, self.made = base, 0


def bass_hybrid_trunk(nc, x, w_in0, w_pool0, w_out0, w_in1, w_out1, gain_rows, qk_gains, table, pool_table, eye, out):
    with ExitStack() as ctx:
        def sb(name, shape, dt=F32):
            return ctx.enter_context(nc.sbuf_tensor(name, shape, dt))

        def sem(name):
            return ctx.enter_context(nc.semaphore(name))

        raw = sb("raw", [P, RING, GK * COLS])
        w_hi = sb("w_hi", [P, RING, GK * COLS], F32R)
        w_lo = sb("w_lo", [P, RING, GK * COLS], F32R)
        xs = sb("xs", [P, TT, D_MODEL])
        hT_hi = sb("hT_hi", [P, KD, SEQ], F32R)
        hT_lo = sb("hT_lo", [P, KD, SEQ], F32R)
        aT_hi = sb("aT_hi", [P, KI, SEQ], F32R)
        aT_lo = sb("aT_lo", [P, KI, SEQ], F32R)
        wide = sb("wide", [P, TT, D_INNER])
        u_hi = sb("u_hi", [P, TT, COLS], F32R)
        u_lo = sb("u_lo", [P, TT, COLS], F32R)
        pool_mat = sb("pool_mat", [P, POOL_COLS], F32R)
        edge_hi = sb("edge_hi", [P, GROUPS, EDGE], F32R)
        ysb = sb("ysb", [P, 2, TT, COLS])
        k_s = sb("k_s", [P, TT, COLS])
        qT = sb("qT", [P, HPG, SEQ])
        kT = sb("kT", [P, HPG, SEQ])
        probs = sb("probs", [P, 3 * P])
        probsT = sb("probsT", [P, 3 * P])
        rope_tab = sb("rope_tab", [P, 4, TT, HEAD_DIM])
        ident = sb("ident", [P, P])
        ident_b = sb("ident_b", [P, P], BF16)
        mask_b = sb("mask_b", [P, P], BF16)
        vec_rows = qT[0:32, 0, 0:P]
        gains = sb("gains", [P, 2 * KD + KI])
        sumsq = sb("sumsq", [P, TT, 2])
        mean = sb("mean", [P, TT])
        rstd = sb("rstd", [P, TT])
        rstd_half = sb("rstd_half", [P, TT])
        minus_half = sb("minus_half", [P, 8])
        head_eps = sb("head_eps", [P, TT, HPG])
        head_root = sb("head_root", [P, TT, HPG])
        qk_sum = sb("qk_sum", [P, 2, TT, HPG])
        qk_mean = sb("qk_mean", [P, 2, TT, HPG])
        qk_rstd = sb("qk_rstd", [P, 2, TT, HPG])
        row_max = sb("row_max", [P, HPG, TT])
        exp_bias = sb("exp_bias", [P, HPG, TT])
        row_sum = sb("row_sum", [P, HPG, TT])
        row_inv = sb("row_inv", [P, HPG, TT])
        o_scale = sb("o_scale", [P, HPG, TT])

        pool_mats = k_s[:, :, :].rearrange("p t n -> p (t n)")[:, 0:GROUPS * POOL_COLS].rearrange(
            "p (g n) -> p g n", g=GROUPS)

        gate1 = wide[:, :, 0:COLS]
        scratch = [wide[:, :, COLS:2 * COLS], wide[:, :, 2 * COLS:3 * COLS]]
        qk = [wide[:, :, 3 * COLS:4 * COLS], k_s[:, :, :]]
        y1 = ysb[:, 0]
        v_s = ysb[:, 1]
        staged = wide[:, :, :].rearrange("p t n -> p (t n)")
        gain_q = staged[:, C_END:C_END + HEAD_DIM]
        gain_k = staged[:, C_END + HEAD_DIM:C_END + 2 * HEAD_DIM]

        acc = [[ctx.enter_context(nc.psum_tensor(f"acc{b}{t}", [P, COLS], F32)) for t in range(TT)] for b in range(2)]
        aux = [ctx.enter_context(nc.psum_tensor(f"aux{i}", [P, COLS], F32)) for i in range(4)]

        raw_landed = [sem(f"raw_landed{i}") for i in range(RING)]
        eye_landed, gains_landed, table_landed = sem("eye_landed"), sem("gains_landed"), sem("table_landed")
        x_landed = [sem(f"x_landed{h}") for h in range(2)]
        piece_landed = [sem(f"piece_landed{i}") for i in range(GK - 1)]
        piece_hi, piece_split = sem("piece_hi"), sem("piece_split")
        hi_first = sem("hi_first")
        hi_made = sem("hi_made")
        w_split = sem("w_split")
        w_used = sem("w_used")
        tile0_ready = sem("tile0_ready")
        gains_turned, gains_made = sem("gains_turned"), sem("gains_made")
        tables_made, poolmat_made, poolmat_placed = sem("tables_made"), sem("poolmat_made"), sem("poolmat_placed")
        sumsq_made, rstd_made = sem("sumsq_made"), sem("rstd_made")
        h_turned, h_hi, h_split = sem("h_turned"), sem("h_hi"), sem("h_split")
        u_hi_made, u_split = sem("u_hi_made"), sem("u_split")
        pooled, pooled_hi, pooled_split = sem("pooled"), sem("pooled_hi"), sem("pooled_split")
        tanh_made, gate_made = sem("tanh_made"), sem("gate_made")
        y0_made = sem("y0_made")
        y_turned, y_hi, y_split = sem("y_turned"), sem("y_hi"), sem("y_split")
        x1_made = sem("x1_made")
        qkv_out = [sem("q_out"), sem("k_out"), sem("v_out")]
        squared = [sem("q_squared"), sem("k_squared")]
        summed = [sem("q_summed"), sem("k_summed")]
        qk_scaled = sem("qk_scaled")
        rope_parts = [sem("q_rope_parts"), sem("k_rope_parts")]
        roped = [sem("q_roped"), sem("k_roped")]
        qk_turned = [sem("q_turned"), sem("k_turned")]
        qkT_made = [sem("qT_made"), sem("kT_made")]
        scores_ready, bias_made, exp_made = sem("scores_ready"), sem("bias_made"), sem("exp_made")
        p_turned, pT_made, o_ready, y1_made = sem("p_turned"), sem("pT_made"), sem("o_ready"), sem("y1_made")
        out_made, out_stored = sem("out_made"), sem("out_stored")
        dve_chain, pool_chain, act_chain = sem("dve_chain"), sem("pool_chain"), sem("act_chain")

        block = ctx.enter_context(nc.Block())

        def product_ready(eng, t, i, n):
            if t == 0:
                eng.wait_ge(tile0_ready, i + 1)
            else:
                eng.wait_ge(w_used, n + 1)

        w_in0_v = w_in0.rearrange("(k p) n -> p k n", p=P)
        w_out0_v = w_out0.rearrange("(k p) n -> p k n", p=P)
        w_in1_v = w_in1.rearrange("(k p) n -> p k n", p=P)
        w_out1_v = w_out1.rearrange("(k p) n -> p k n", p=P)

        @block.sync
        def _(sp):
            def load(slot, src, n=None):
                if n is not None:
                    sp.wait_ge(w_split, n - RING + 1)
                sp.dma_start(raw[:, slot, :].rearrange("p (k n) -> p k n", k=GK), src).then_inc(raw_landed[slot], 16)

            def load_in0(g, first=False):
                for j in range(1 if first else 0, 4):
                    src = w_in0_v[:, (j % 2) * GK:(j % 2 + 1) * GK, bass.ds((j // 2) * D_INNER + g * COLS, COLS)]
                    load(j, src, None if first else 4 * g + j)

            for half in range(2):
                c = slice(half * COLS, (half + 1) * COLS)
                sp.dma_start(xs[:, :, c], x[0].rearrange("(t p) n -> p t n", p=P)[:, :, c]).then_inc(x_landed[half], 16)
            for k in range(GK):
                sp.dma_start(raw[:, 0, k * COLS:(k + 1) * COLS],
                             w_in0_v[:, k, 0:COLS]).then_inc((*piece_landed, raw_landed[0])[k], 16)
            load_in0(0, first=True)
            with sp.Fori(1, GROUPS) as g:
                load_in0(g)
            for g in range(GROUPS):
                load(g, w_pool0[g].rearrange("(k p) n -> p k n", p=P), N_POOL + g)
            for h in range(2):
                for q in range(4):
                    load(q, w_out0_v[:, q * GK:(q + 1) * GK, h * COLS:(h + 1) * COLS], N_OUT0 + 4 * h + q)
            with sp.Fori(0, GROUPS) as g:
                for j in range(8):
                    src = w_in1_v[:, (j % 2) * GK:(j % 2 + 1) * GK, bass.ds((j // 2) * D_INNER + g * COLS, COLS)]
                    load(j % RING, src, N_L1 + 8 * g + j)
            for i, (h, q) in enumerate(OUT1_ORDER):
                load(i % RING, w_out1_v[:, q * GK:(q + 1) * GK, h * COLS:(h + 1) * COLS], N_OUT1 + i)
            for i in range(2 * TT):
                h, t = i // TT, i % TT
                sp.wait_ge(out_made, i + 1)
                sp.dma_start(out[0, t * P:(t + 1) * P, h * COLS:(h + 1) * COLS],
                             ysb[:, h, t, :]).then_inc(out_stored, 16)
            sp.wait_ge(out_stored, 16 * 2 * TT)

        @block.gpsimd
        def _(pool):
            chain = Chain(pool, pool_chain)
            chain.done(pool.memset(minus_half[:, :], -0.5))
            chain.done(pool.memset(head_eps[:, :, :], HEAD_DIM * EPS))
            chain.done(pool.memset(head_root[:, :, :], HEAD_DIM ** 0.5))
            for k in range(GK):
                piece = slice(k * COLS, (k + 1) * COLS)
                pool.wait_ge((*piece_landed, raw_landed[0])[k], 16)
                pool.tensor_scalar(w_hi[:, 0, piece], raw[:, 0, piece], 1.0, 1.0, ALU.mult,
                                   ALU.mult).then_inc(piece_hi, 1)
            for n in range(1, RING - 1):
                pool.wait_ge(raw_landed[n], 16)
                pool.tensor_scalar(w_hi[:, n, :], raw[:, n, :], 1.0, 1.0, ALU.mult, ALU.mult).then_inc(hi_first, 1)

            def row_norm(times):
                pool.wait_ge(sumsq_made, 2 * TT * times)
                chain.done(pool.tensor_tensor(mean[:, :], sumsq[:, :, 0], sumsq[:, :, 1], ALU.add))
                chain.done(pool.tensor_scalar(mean[:, :], mean[:, :], 1.0 / D_MODEL, EPS, ALU.mult, ALU.add))
                chain.done(pool.tensor_tensor(rstd[:, :], mean[:, :], minus_half[:, 0:TT], ALU.pow))
                pool.tensor_scalar(rstd_half[:, :], rstd[:, :], 0.5, 1.0, ALU.mult, ALU.mult).then_inc(rstd_made, 1)

            row_norm(1)
            pool.wait_ge(table_landed, 3 * 16)
            edge = pool_mats[:, :, BAND:BAND + EDGE]
            chain.done(pool.tensor_scalar(edge_hi[:, :, :], edge, 1.0, 1.0, ALU.mult, ALU.mult))
            pool.tensor_tensor(pool_mats[:, :, BAND + EDGE:], edge, edge_hi[:, :, :].bitcast(F32),
                               ALU.subtract).then_inc(poolmat_made, 1)
            pool.tensor_copy(mask_b[:, :], staged[:, C_MASK:C_END])
            pool.wait_ge(eye_landed, 16)
            pool.tensor_copy(ident_b[:, :], ident[:, :])
            half = HEAD_DIM // 2
            for i, gain in enumerate((gain_q, gain_k)):
                for t in range(TT):
                    cos = staged[:, C_COS + t * HEAD_DIM:C_COS + (t + 1) * HEAD_DIM]
                    sin = staged[:, C_SIN + t * HEAD_DIM:C_SIN + (t + 1) * HEAD_DIM]
                    pool.tensor_tensor(rope_tab[:, 2 * i, t, :], cos, gain, ALU.mult)
                    pool.tensor_tensor(rope_tab[:, 2 * i + 1, t, 0:half], sin[:, 0:half], gain[:, half:], ALU.mult)
                    last = pool.tensor_tensor(rope_tab[:, 2 * i + 1, t, half:], sin[:, half:], gain[:, 0:half],
                                              ALU.mult)
            last.then_inc(tables_made, 1)
            row_norm(2)

            def norm_rope(g, i, first=False):
                v = qk[i]
                pool.wait_ge(qkv_out[i], TT * (g + 1))
                pool.tensor_tensor(scratch[i], v, v, ALU.mult).then_inc(squared[i], 1)
                pool.wait_ge(summed[i], g + 1)
                chain.done(pool.tensor_tensor(qk_mean[:, i], qk_sum[:, i], head_eps[:, :, :], ALU.add))
                if i == 0 and not first:
                    pool.wait_ge(exp_made, HPG * g)
                scaled = pool.tensor_tensor(qk_rstd[:, i], qk_mean[:, i],
                                            minus_half[:, :].rearrange("p (t h) -> p t h", t=TT), ALU.pow)
                if i == 0:
                    scaled.then_inc(qk_scaled, 1)
                else:
                    chain.done(scaled)
                    chain.done(pool.tensor_tensor(qk_rstd[:, i], qk_rstd[:, i], head_root[:, :, :], ALU.mult))
                v4 = v.rearrange("p t (h d) -> p t h d", h=HPG)
                s4 = scratch[i].rearrange("p t (h d) -> p t h d", h=HPG)
                if i == 1:
                    for t in range(TT):
                        ins = pool.tensor_tensor(v4[:, t], v4[:, t],
                                                 qk_rstd[:, i, t, :].unsqueeze(2).to_broadcast([P, HPG, HEAD_DIM]),
                                                 ALU.mult)
                    chain.done(ins)
                for t in range(TT):
                    for a, b in ((0, half), (half, 0)):
                        tab = rope_tab[:, 2 * i + 1, t, a:a + half].unsqueeze(1).to_broadcast([P, HPG, half])
                        ins = pool.tensor_tensor(s4[:, t, :, a:a + half], v4[:, t, :, b:b + half], tab, ALU.mult)
                chain.done(ins)
                for t in range(TT):
                    tab = rope_tab[:, 2 * i, t, :].unsqueeze(1).to_broadcast([P, HPG, HEAD_DIM])
                    ins = pool.tensor_tensor(v4[:, t], v4[:, t], tab, ALU.mult)
                ins.then_inc(rope_parts[i], 1)

            start, per_group = chain.made, 7
            norm_rope(0, 0, first=True)
            norm_rope(0, 1, first=True)
            with pool.Fori(1, GROUPS) as g:
                chain.rebase(start + per_group * g)
                norm_rope(g, 0)
                norm_rope(g, 1)
                assert chain.made == per_group, chain.made

        @block.scalar
        def _(act):
            act.dma_start(ident[:, :], eye).then_inc(eye_landed, 16)
            act.dma_start(vec_rows, gain_rows).then_inc(gains_landed, 16)
            act.wait_ge(x_landed[0], 16)
            act.dma_start(pool_mats.rearrange("p g n -> p (g n)"), pool_table).then_inc(table_landed, 16)
            act.dma_start(staged[:, 0:C_END], table).then_inc(table_landed, 16)
            act.dma_start(staged[:, C_END:C_END + 2 * HEAD_DIM],
                          qk_gains.partition_broadcast(P)).then_inc(table_landed, 16)

            def weight_hi(n, slot, landed):
                act.wait_ge(raw_landed[slot], landed)
                act.wait_ge(w_used, n - RING + 1)
                act.activation(w_hi[:, slot, :], raw[:, slot, :], ACT.Copy).then_inc(hi_made, 1)

            def static_hi(n):
                weight_hi(n, n % RING, 16 * (n // RING + 1))

            def turned_hi(dst, f0, bank, turned, made, gain=None):
                act.wait_ge(turned[0], turned[1])
                if gain is None:
                    act.activation(dst[:, bass.ds(f0, 2), :].rearrange("p f s -> p (f s)"), aux[bank][:, :],
                                   ACT.Copy).then_inc(made, 1)
                    return
                for j in range(2):
                    ins = act.activation(dst[:, f0 + j, :], aux[bank][:, j * SEQ:(j + 1) * SEQ], ACT.Copy,
                                         scale=gains[:, gain + f0 + j:gain + f0 + j + 1])
                ins.then_inc(made, 1)

            def squares(t, half):
                act.activation(ysb[:, half, t], xs[:, t, half * COLS:(half + 1) * COLS], ACT.Square,
                               accum_out=sumsq[:, t, half:half + 1]).then_inc(sumsq_made, 1)

            act.wait_ge(gains_turned, 1)
            act.activation(gains[:, :], aux[3][:, 0:2 * KD + KI], ACT.Copy).then_inc(gains_made, 1)
            act.wait_ge(gains_made, 1)
            for b in range(KD // 2):
                turned_hi(hT_hi, 2 * b, b, (h_turned, b + 1), h_hi, gain=0)
            act.wait_ge(x_landed[1], 16)
            for t in range(TT):
                for half in range(2):
                    squares(t, half)

            act.wait_ge(raw_landed[3], 16)
            act.activation(w_hi[:, 3, :], raw[:, 3, :], ACT.Copy).then_inc(hi_made, 1)

            with act.Fori(0, GROUPS) as g:
                weight_hi(4 * g + 4, 0, 16 * (g + 2))
                act.wait_ge(rstd_made, 1)
                act.wait_ge(poolmat_made, 1)
                product_ready(act, 0, 2 * g, 4 * g + 1)
                act.activation(pool_mat[:, :], pool_mats[:, g, :], ACT.Copy).then_inc(poolmat_placed, 1)
                for t in range(TT):
                    product_ready(act, t, 2 * g, 4 * g + 1)
                    act.activation(u_hi[:, t, :], acc[0][t][:, :], ACT.Copy,
                                   scale=rstd[:, t:t + 1]).then_inc(u_hi_made, 1)
                weight_hi(4 * g + 5, 1, 16 * (g + 2))
                for b in range(2):
                    turned_hi(aT_hi, HPG * g + 2 * b, b, (pooled, 2 * g + b + 1), pooled_hi)
                weight_hi(4 * g + 6, 2, 16 * (g + 2))
                act.wait_ge(tables_made, 1)
                for t in range(TT):
                    product_ready(act, t, 2 * g + 1, 4 * g + 3)
                    act.activation(wide[:, t, bass.ds(g * COLS, COLS)], acc[1][t][:, :], ACT.Tanh,
                                   scale=rstd_half[:, t:t + 1]).then_inc(tanh_made, 1)
                weight_hi(4 * g + 7, 3, 16 * (g + 2))

            def y0_hi(g):
                for b in range(2):
                    turned_hi(aT_hi, HPG * g + 2 * b, 2 * (g % 2) + b, (y_turned, 2 * g + b + 1), y_hi, gain=2 * KD)

            for g in range(GROUPS):
                if g > 0:
                    static_hi(N_POOL + 3 + g)
                    y0_hi(g - 1)
            static_hi(N_OUT0 + 3)
            y0_hi(GROUPS - 1)

            def h1_hi(half):
                for t in range(TT):
                    act.wait_ge(x1_made, TT * half + t + 1)
                    if half == 0 and t == 0:
                        act.wait_ge(rstd_made, 1)
                    squares(t, half)
                for b in range(2):
                    turned_hi(hT_hi, 4 * half + 2 * b, 2 * half + b, (h_turned, 4 + 2 * half + b + 1), h_hi, gain=KD)

            for n in range(N_OUT0 + 4, N_OUT0 + 8):
                static_hi(n)
            h1_hi(0)
            for n in range(N_OUT0 + 8, N_L1 + 3):
                static_hi(n)

            def exp_scores(g, h):
                act.wait_ge(bias_made, HPG * g + h + 1)
                if h > 0:
                    act.wait_ge(p_turned, HPG * g + h)
                act.activation(probs[:, 0:P], aux[h % 2][:, 0:P], ACT.Exp, bias=exp_bias[:, h, 0:1],
                               scale=qk_rstd[:, 0, 0, h:h + 1], accum_out=row_sum[:, h, 0:1])
                act.activation(probs[:, P:3 * P], aux[h % 2][:, P:3 * P], ACT.Exp, bias=exp_bias[:, h, 1:2],
                               scale=qk_rstd[:, 0, 1, h:h + 1], accum_out=row_sum[:, h, 1:2]).then_inc(exp_made, 1)

            def probs_out(g, h):
                act.wait_ge(p_turned, HPG * g + h + 1)
                if h > 0:
                    act.wait_ge(o_ready, HPG * g + h)
                act.activation(probsT[:, :], aux[2][:, 0:3 * P], ACT.Copy).then_inc(pT_made, 1)

            def qkv_evacuate(g, which, first=False):
                if first:
                    pass
                elif which < 2:
                    act.wait_ge(qk_turned[which], 2 * g)
                else:
                    act.wait_ge(o_ready, HPG * g)
                dst = (*qk, v_s)[which]
                for t in range(TT):
                    product_ready(act, t, 14 + 4 * g + which, N_L1 + 8 * g + 2 * which + 1)
                    ins = act.activation(dst[:, t, :], acc[which % 2][t][:, :], ACT.Copy, scale=rstd[:, t:t + 1])
                    ins.then_inc(qkv_out[which], 1)

            def qkT_out(g, i):
                for b in range(2):
                    act.wait_ge(qk_turned[i], 2 * g + b + 1)
                    dst = (qT, kT)[i]
                    act.activation(dst[:, 2 * b:2 * b + 2, :].rearrange("p h s -> p (h s)"), aux[2 * i + b][:, :],
                                   ACT.Copy).then_inc(qkT_made[i], 1)

            def tanh_z(g, first):
                for t in range(TT):
                    product_ready(act, t, 17 + 4 * g, N_L1 + 8 * g + 7)
                    if not first:
                        act.wait_ge(y1_made, HPG * g)
                    act.activation(gate1[:, t, :], acc[1][t][:, :], ACT.Tanh,
                                   scale=rstd_half[:, t:t + 1]).then_inc(tanh_made, 1)

            def y1_hi(g):
                for b in range(2):
                    turned_hi(aT_hi, HPG * g + 2 * b, b, (y_turned, 8 + 2 * g + b + 1), y_hi)

            def layer1(g, attend):
                def w(j):
                    weight_hi(N_L1 + 3 + 8 * g + j, (N_L1 + 3 + j) % RING, 16 * ((N_L1 + 3 + j) // RING + 1) + 32 * g)
                w(0)
                if attend:
                    exp_scores(g - 1, 0)
                qkv_evacuate(g, 0, not attend)
                w(1)
                if attend:
                    exp_scores(g - 1, 1)
                    probs_out(g - 1, 0)
                w(2)
                if attend:
                    exp_scores(g - 1, 2)
                    probs_out(g - 1, 1)
                qkv_evacuate(g, 1, not attend)
                w(3)
                if attend:
                    exp_scores(g - 1, 3)
                    probs_out(g - 1, 2)
                w(4)
                if attend:
                    probs_out(g - 1, 3)
                w(5)
                qkv_evacuate(g, 2, not attend)
                w(6)
                qkT_out(g, 0)
                w(7)
                tanh_z(g, not attend)
                if attend:
                    y1_hi(g - 1)
                qkT_out(g, 1)

            h1_hi(1)
            act.wait_ge(rstd_made, 2)
            layer1(0, attend=False)
            with act.Fori(1, GROUPS) as g:
                layer1(g, attend=True)

            last = GROUPS - 1
            for n in range(N_OUT1 + 3, N_END):
                static_hi(n)
                j = n - N_OUT1 - 3
                if j < HPG:
                    exp_scores(last, j)
                if 1 <= j <= HPG:
                    probs_out(last, j - 1)
            y1_hi(last)

        @block.tensor
        def _(pe):
            def granule(n, slot, buf, free, src_hi, src_lo, k0, first, last, need=None, mid=None):
                if first and free:
                    pe.wait_ge(*free)
                if not (isinstance(n, int) and n == 0):
                    pe.wait_ge(w_split, n + 1)
                order = [(t, k) for t in range(TT) for k in range(GK)] if last and not mid and not need else \
                    [(t, k) for k in range(GK) for t in range(TT)]
                for i, (t, k) in enumerate(order):
                    if mid and i == 2 * TT:
                        mid()
                    if need and t == 0:
                        need(k0 + k)
                    if isinstance(n, int) and n == 0 and t == 0:
                        pe.wait_ge(*((piece_split, k + 1) if k < GK - 1 else (w_split, 1)))
                    whi = w_hi[:, slot, k * COLS:(k + 1) * COLS]
                    wlo = w_lo[:, slot, k * COLS:(k + 1) * COLS]
                    shi = src_hi[:, k0 + k, t * P:(t + 1) * P]
                    slo = src_lo[:, k0 + k, t * P:(t + 1) * P]
                    a = acc[buf][t][:, :]
                    pe.matmul(a, shi, whi, start=first and k == 0, stop=False)
                    pe.matmul(a, shi, wlo, start=False, stop=False)
                    ins = pe.matmul(a, slo, whi, start=False, stop=last and k == GK - 1)
                    if last and k == GK - 1 and t == 0:
                        ins.then_inc(tile0_ready, 1)
                    if i == TT * GK - 1:
                        ins.then_inc(w_used, 1)

            def turn(dst_banks, src, made, tiles=range(HPG)):
                for f in tiles:
                    for t in range(TT):
                        c = (f % 2) * SEQ + t * P
                        ins = pe.transpose(aux[dst_banks[f // 2]][:, c:c + P], src[:, t, f * P:(f + 1) * P],
                                           ident[:, :])
                    if f % 2:
                        ins.then_inc(made, 1)

            pe.wait_ge(eye_landed, 16)
            pe.wait_ge(gains_landed, 16)
            pe.transpose(aux[3][:, 0:32], vec_rows, ident[0:32, 0:32]).then_inc(gains_turned, 1)
            pe.wait_ge(x_landed[0], 16)
            turn((0, 1), xs[:, :, 0:COLS], h_turned)

            def turn_x_rest():
                pe.wait_ge(x_landed[1], 16)
                pe.wait_ge(gains_made, 1)
                turn((2, 3), xs[:, :, COLS:], h_turned)

            def h_needed(base):
                def need(k):
                    if k % 2 == 0:
                        pe.wait_ge(h_split, base + k // 2 + 1)
                return need

            def pool_tokens(g):
                pe.wait_ge(poolmat_placed, g + 1)
                pe.wait_ge(u_split, TT * (g + 1))
                for f in range(HPG):
                    bank, c = aux[f // 2], (f % 2) * SEQ
                    for t in range(TT):
                        for part in (u_hi, u_lo):
                            lhs = part[:, t, f * P:(f + 1) * P]
                            if t == 0:
                                pe.matmul(bank[:, c:c + EDGE], lhs, pool_mat[:, BAND:BAND + EDGE], start=part is u_hi, stop=False,
                                          skip_group_check=True)
                                pe.matmul(bank[:, c:c + EDGE], lhs, pool_mat[:, BAND + EDGE:], start=False, stop=False,
                                          skip_group_check=True)
                                pe.matmul(bank[:, c + EDGE:c + BAND], lhs, pool_mat[:, EDGE:BAND], start=False,
                                          stop=False, skip_group_check=True)
                            else:
                                ins = pe.matmul(bank[:, c + P:c + 2 * P], lhs, pool_mat[:, 0:P], start=False,
                                                stop=True, skip_group_check=True)
                    if f % 2:
                        ins.then_inc(pooled, 1)

            def layer0(g, first):
                for j in range(4):
                    granule(4 * g + j, j, j // 2, None, hT_hi, hT_lo, GK * (j % 2), first=j % 2 == 0, last=j % 2 == 1,
                            need=h_needed(0) if first and j < 2 else None,
                            mid=turn_x_rest if first and j == 0 else None)
                    if j == 2:
                        pool_tokens(g)

            layer0(0, first=True)
            with pe.Fori(1, GROUPS) as g:
                layer0(g, first=False)

            def turn_y0(g):
                pe.wait_ge(y0_made, g + 1)
                if g >= 2:
                    pe.wait_ge(y_split, 2 * (g - 1))
                turn((2 * (g % 2), 2 * (g % 2) + 1), ysb[:, g % 2], y_turned)

            pe.wait_ge(pooled_split, 2 * GROUPS)
            for g in range(GROUPS):
                free = (y0_made, g - 1) if g >= 2 else ((u_split, gate_made)[g], TT * GROUPS)
                granule(N_POOL + g, g, g % 2, free, aT_hi, aT_lo, HPG * g, first=True, last=True)
                if g > 0:
                    turn_y0(g - 1)

            def turn_x1(half):
                pe.wait_ge(x1_made, TT * (half + 1))
                turn((2 * half, 2 * half + 1), xs[:, :, half * COLS:(half + 1) * COLS], h_turned)

            for half in range(2):
                for q in range(4):
                    pe.wait_ge(y_split, 2 * (q + 1))
                    granule(N_OUT0 + 4 * half + q, q, half, (y0_made, 3 + half), aT_hi, aT_lo, GK * q, first=q == 0, last=q == 3)
                    if (half, q) == (0, 0):
                        turn_y0(GROUPS - 1)
                    if (half, q) == (1, 0):
                        turn_x1(0)

            pe.wait_ge(tables_made, 1)

            def scores(g, h):
                for i in range(2):
                    pe.wait_ge(qkT_made[i], 2 * (g + 1))
                if h < 2:
                    pe.wait_ge(y_split, 8 + 2 * g)
                else:
                    pe.wait_ge(exp_made, HPG * g + h - 1)
                s = aux[h % 2]
                pe.matmul(s[:, 0:P], ident_b[:, :], mask_b[:, :], start=True, stop=False)
                pe.matmul(s[:, 0:P], qT[:, h, 0:P], kT[:, h, 0:P], start=False, stop=True)
                pe.matmul(s[:, P:3 * P], qT[:, h, P:SEQ], kT[:, h, :], start=True, stop=False)
                pe.matmul(s[:, 2 * P:3 * P], ident_b[:, :], mask_b[:, :], start=False,
                          stop=True).then_inc(scores_ready, 1)

            def turn_probs(g, h):
                pe.wait_ge(exp_made, HPG * g + h + 1)
                if h > 0:
                    pe.wait_ge(pT_made, HPG * g + h)
                for i in range(3):
                    ins = pe.transpose(aux[2][:, i * P:(i + 1) * P], probs[:, i * P:(i + 1) * P], ident[:, :])
                ins.then_inc(p_turned, 1)

            def values(g, h):
                pe.wait_ge(pT_made, HPG * g + h + 1)
                pe.wait_ge(qkv_out[2], TT * (g + 1))
                if h > 0:
                    pe.wait_ge(y1_made, HPG * g + h)
                v = [v_s[:, t, h * P:(h + 1) * P] for t in range(TT)]
                pe.matmul(aux[3][:, 0:P], probsT[:, 0:P], v[0], start=True, stop=True)
                pe.matmul(aux[3][:, P:2 * P], probsT[:, P:2 * P], v[0], start=True, stop=False)
                pe.matmul(aux[3][:, P:2 * P], probsT[:, 2 * P:3 * P], v[1], start=False,
                          stop=True).then_inc(o_ready, 1)

            def turn_qk(g, i, first):
                pe.wait_ge(roped[i], g + 1)
                if first:
                    pass
                elif i == 0:
                    pe.wait_ge(exp_made, HPG * g)
                else:
                    pe.wait_ge(y1_made, HPG * g)
                turn((2 * i, 2 * i + 1), qk[i], qk_turned[i])

            def turn_y1(g, after_q):
                pe.wait_ge(y1_made, HPG * (g + 1))
                if after_q is not None:
                    pe.wait_ge(qkT_made[0], 2 * (after_q + 1))
                turn((0, 1), y1, y_turned)

            def attend(g, j):
                if j < HPG:
                    scores(g, j)
                if 2 <= j < HPG + 2:
                    values(g, j - 2)
                if 1 <= j < HPG + 1:
                    turn_probs(g, j - 1)

            def layer1(g, first):
                for j in range(8):
                    which = j // 2
                    free = {0: (x1_made, TT) if first else (qkv_out[2], TT * g),
                            1: (x1_made, 2 * TT) if first else (gate_made, TT * (GROUPS + g)),
                            2: (qkv_out[0], TT * (g + 1)), 3: (qkv_out[1], TT * (g + 1))}[which]
                    granule(N_L1 + 8 * g + j, j % RING, which % 2, free, hT_hi, hT_lo,
                            GK * (j % 2), first=j % 2 == 0, last=j % 2 == 1,
                            need=h_needed(4) if first and j < 2 else None,
                            mid=(lambda: turn_x1(1)) if first and j == 0 else None)
                    if not first:
                        attend(g - 1, j)
                    if j == 6:
                        turn_qk(g, 0, first)
                    if j == 7:
                        if not first:
                            turn_y1(g - 1, g)
                        turn_qk(g, 1, first)

            layer1(0, first=True)
            with pe.Fori(1, GROUPS) as g:
                layer1(g, first=False)

            last = GROUPS - 1

            def turn_y1_last(b):
                pe.wait_ge(y1_made, HPG * last + 2 * b + 2)
                pe.wait_ge(exp_made, HPG * last + 3 + b)
                turn((0, 1), y1, y_turned, tiles=(2 * b, 2 * b + 1))

            def y_needed(k):
                if k % 2 == 0:
                    pe.wait_ge(y_split, 8 + k // 2 + 1)

            for j, (half, q) in enumerate(OUT1_ORDER):
                granule(N_OUT1 + j, j % RING, half, ((qkv_out[2], TT * GROUPS), (gate_made, 2 * TT * GROUPS))[half],
                        aT_hi, aT_lo, GK * q, first=q == 0, last=q == 3, need=y_needed if j < 7 else None,
                        mid=(lambda: turn_y1_last(1)) if j == 6 else None)
                attend(last, j)
                if j == 4:
                    turn_y1_last(0)

        @block.vector
        def _(dve):
            chain = Chain(dve, dve_chain)

            def weight_lo(n, slot):
                dve.wait_ge(hi_made, n - RING + 2)
                dve.tensor_tensor(w_lo[:, slot, :], raw[:, slot, :], w_hi[:, slot, :].bitcast(F32),
                                  ALU.subtract).then_inc(w_split, 1)

            def turned_lo(dst, hi_src, f0, bank, hi_sem, hi_count, made, gain=None):
                dve.wait_ge(hi_sem, hi_count)
                if gain is None:
                    dve.tensor_tensor(dst[:, bass.ds(f0, 2), :].rearrange("p f s -> p (f s)"), aux[bank][:, :],
                                      hi_src[:, bass.ds(f0, 2), :].bitcast(F32).rearrange("p f s -> p (f s)"),
                                      ALU.subtract).then_inc(made, 1)
                    return
                for j in range(2):
                    ins = dve.scalar_tensor_tensor(dst[:, f0 + j, :], aux[bank][:, j * SEQ:(j + 1) * SEQ],
                                                   gains[:, gain + f0 + j:gain + f0 + j + 1],
                                                   hi_src[:, f0 + j, :].bitcast(F32), ALU.mult, ALU.subtract)
                ins.then_inc(made, 1)

            def first_lo(n):
                dve.wait_ge(hi_first, n)
                dve.tensor_tensor(w_lo[:, n, :], raw[:, n, :], w_hi[:, n, :].bitcast(F32),
                                  ALU.subtract).then_inc(w_split, 1)

            def piece_lo(k):
                piece = slice(k * COLS, (k + 1) * COLS)
                dve.wait_ge(piece_hi, k + 1)
                dve.tensor_tensor(w_lo[:, 0, piece], raw[:, 0, piece], w_hi[:, 0, piece].bitcast(F32),
                                  ALU.subtract).then_inc(piece_split if k < GK - 1 else w_split, 1)

            def h0_lo(b):
                turned_lo(hT_lo, hT_hi, 2 * b, b, h_hi, b + 1, h_split, gain=0)

            h0_lo(0)
            piece_lo(0)
            piece_lo(1)
            h0_lo(1)
            piece_lo(2)
            piece_lo(3)
            h0_lo(2)
            first_lo(1)
            h0_lo(3)
            first_lo(2)
            weight_lo(3, 3)

            with dve.Fori(0, GROUPS) as g:
                weight_lo(4 * g + 4, 0)
                dve.wait_ge(rstd_made, 1)
                for t in range(TT):
                    dve.wait_ge(u_hi_made, TT * g + t + 1)
                    ins = dve.scalar_tensor_tensor(u_lo[:, t, :], acc[0][t][:, :], rstd[:, t:t + 1],
                                                   u_hi[:, t, :].bitcast(F32), ALU.mult, ALU.subtract)
                    ins.then_inc(u_split, 1)
                weight_lo(4 * g + 5, 1)
                for b in range(2):
                    turned_lo(aT_lo, aT_hi, HPG * g + 2 * b, b, pooled_hi, 2 * g + b + 1, pooled_split)
                for t in range(TT):
                    dve.wait_ge(tanh_made, TT * g + t + 1)
                    gate = wide[:, t, bass.ds(g * COLS, COLS)]
                    ins = dve.scalar_tensor_tensor(gate, gate, 1.0, acc[1][t][:, :], ALU.add, ALU.mult)
                    ins.then_inc(gate_made, 1)
                weight_lo(4 * g + 6, 2)
                weight_lo(4 * g + 7, 3)

            def y0_lo(g):
                for b in range(2):
                    turned_lo(aT_lo, aT_hi, HPG * g + 2 * b, 2 * (g % 2) + b, y_hi, 2 * g + b + 1, y_split,
                              gain=2 * KD)

            dve.wait_ge(gate_made, TT * GROUPS)
            for g in range(GROUPS):
                n = N_POOL + 3 + g
                if g > 0:
                    weight_lo(n, n % RING)
                for t in range(TT):
                    product_ready(dve, t, 8 + g, N_POOL + g)
                    if g >= 2:
                        dve.wait_ge(y_turned, 2 * (g - 1))
                    ins = dve.scalar_tensor_tensor(ysb[:, g % 2, t, :], acc[g % 2][t][:, :], rstd_half[:, t:t + 1],
                                                   wide[:, t, g * COLS:(g + 1) * COLS], ALU.mult, ALU.mult)
                    if t == TT - 1:
                        ins.then_inc(y0_made, 1)
                if g > 0:
                    y0_lo(g - 1)
            weight_lo(N_OUT0 + 3, (N_OUT0 + 3) % RING)
            y0_lo(GROUPS - 1)

            def x1(half):
                for t in range(TT):
                    product_ready(dve, t, 12 + half, N_OUT0 + 4 * half + 3)
                    s = xs[:, t, half * COLS:(half + 1) * COLS]
                    ins = dve.tensor_tensor(s, acc[half][t][:, :], s, ALU.add)
                    ins.then_inc(x1_made, 1)

            def h1_lo(half):
                for b in range(2):
                    turned_lo(hT_lo, hT_hi, 4 * half + 2 * b, 2 * half + b, h_hi, 4 + 2 * half + b + 1, h_split,
                              gain=KD)

            for n in range(N_OUT0 + 4, N_OUT0 + 7):
                weight_lo(n, n % RING)
            x1(0)
            weight_lo(N_OUT0 + 7, (N_OUT0 + 7) % RING)
            h1_lo(0)
            for n in range(N_OUT0 + 8, N_L1 + 3):
                weight_lo(n, n % RING)
            x1(1)

            def head_max(g, h):
                dve.wait_ge(scores_ready, HPG * g + h + 1)
                s = aux[h % 2]
                dve.tensor_reduce(row_max[:, h, 0:1], s[:, 0:P], AX_X, ALU.max)
                chain.done(dve.tensor_reduce(row_max[:, h, 1:2], s[:, P:3 * P], AX_X, ALU.max))
                dve.wait_ge(qk_scaled, g + 1)
                dve.scalar_tensor_tensor(exp_bias[:, h, :], row_max[:, h, :], -1.0, qk_rstd[:, 0, :, h],
                                         ALU.mult, ALU.mult).then_inc(bias_made, 1)

            def head_out(g, h):
                dve.wait_ge(exp_made, HPG * g + h + 1)
                chain.done(dve.reciprocal(row_inv[:, h, :], row_sum[:, h, :]))
                chain.done(dve.tensor_tensor(o_scale[:, h, :], row_inv[:, h, :], rstd_half[:, :], ALU.mult))
                dve.wait_ge(o_ready, HPG * g + h + 1)
                dve.wait_ge(y_turned, 8 + 2 * g)
                for t in range(TT):
                    ins = dve.scalar_tensor_tensor(y1[:, t, h * P:(h + 1) * P], aux[3][:, t * P:(t + 1) * P],
                                                   o_scale[:, h, t:t + 1], gate1[:, t, h * P:(h + 1) * P],
                                                   ALU.mult, ALU.mult)
                ins.then_inc(y1_made, 1)

            def sum_squares(g, i):
                dve.wait_ge(squared[i], g + 1)
                dve.tensor_reduce(qk_sum[:, i], scratch[i].rearrange("p t (h d) -> p t h d", h=HPG), AX_X,
                                  ALU.add).then_inc(summed[i], 1)

            def rope_sum(g, i):
                dve.wait_ge(rope_parts[i], g + 1)
                dve.tensor_tensor(qk[i], qk[i], scratch[i], ALU.add).then_inc(roped[i], 1)

            def gate_z(g):
                for t in range(TT):
                    dve.wait_ge(tanh_made, TT * (GROUPS + g) + t + 1)
                    ins = dve.scalar_tensor_tensor(gate1[:, t, :], gate1[:, t, :], 1.0, acc[1][t][:, :],
                                                   ALU.add, ALU.mult)
                    ins.then_inc(gate_made, 1)

            def y1_lo(g):
                for b in range(2):
                    turned_lo(aT_lo, aT_hi, HPG * g + 2 * b, b, y_hi, 8 + 2 * g + b + 1, y_split)

            def layer1(g, attend):
                def w(j):
                    weight_lo(N_L1 + 3 + 8 * g + j, (N_L1 + 3 + j) % RING)
                if attend:
                    head_max(g - 1, 0)
                w(0)
                if attend:
                    head_max(g - 1, 1)
                w(1)
                if attend:
                    dve.wait_ge(gate_made, TT * (GROUPS + g))
                    head_max(g - 1, 2)
                    head_out(g - 1, 0)
                sum_squares(g, 0)
                w(2)
                if attend:
                    head_max(g - 1, 3)
                    head_out(g - 1, 1)
                w(3)
                if attend:
                    head_out(g - 1, 2)
                w(4)
                sum_squares(g, 1)
                rope_sum(g, 0)
                if attend:
                    head_out(g - 1, 3)
                w(5)
                w(6)
                rope_sum(g, 1)
                w(7)
                gate_z(g)
                if attend:
                    y1_lo(g - 1)

            h1_lo(1)
            layer1(0, attend=False)
            start, per_group = chain.made, 3 * HPG
            with dve.Fori(1, GROUPS) as g:
                chain.rebase(start + per_group * (g - 1))
                layer1(g, attend=True)
                assert chain.made == per_group
            chain.rebase(start + per_group * (GROUPS - 1))

            last = GROUPS - 1
            dve.wait_ge(gate_made, TT * 2 * GROUPS)
            for j in range(6):
                if j < HPG:
                    head_max(last, j)
                if j >= 2:
                    head_out(last, j - 2)
                n = N_OUT1 + 3 + j
                if n < N_END:
                    weight_lo(n, n % RING)
            y1_lo(last)
            for half in range(2):
                for t in range(TT):
                    product_ready(dve, t, 30 + half, N_OUT1 + 6 + half)
                    dve.wait_ge(y_turned, 16)
                    dve.tensor_tensor(ysb[:, half, t, :], acc[half][t][:, :], xs[:, t, half * COLS:(half + 1) * COLS],
                                      ALU.add).then_inc(out_made, 1)


_INS = ["x", "w_in0", "w_pool0", "w_out0", "w_in1", "w_out1"]


def kernel(**inputs):
    import concourse.bacc as _bacc
    from concourse import mybir as _mybir
    from concourse.bass_utils import run_bass_kernel_spmd as _run

    nc = _bacc.Bacc("TRN2", target_bir_lowering=False, num_devices=1)
    arrays, args = {}, []
    table, pool_table, eye = constant_tables()
    gain_rows = np.concatenate([np.asarray(inputs[n]) for n in ("norm0", "norm1", "pool_scale0")]).reshape(-1, P)
    qk_gains = np.concatenate([np.asarray(inputs[n]) for n in ("q_norm1", "k_norm1")])
    laid_out = [(n, np.ascontiguousarray(inputs[n])) for n in _INS]
    laid_out += [("gain_rows", gain_rows), ("qk_gains", qk_gains), ("table", table), ("pool_table", pool_table),
                 ("eye", eye)]
    for name, a in laid_out:
        arrays[f"in_{name}_dram"] = a
        args.append(nc.dram_tensor(f"in_{name}_dram", a.shape, _mybir.dt.from_np(a.dtype), kind="ExternalInput").ap())
    args.append(nc.dram_tensor("out_0_dram", (1, SEQ, D_MODEL), F32, kind="ExternalOutput").ap())
    bass_hybrid_trunk(nc, *args)
    r = _run(nc, [arrays], core_ids=[0])
    return r.results[0]["out_0_dram"]
```

```python
from contextlib import ExitStack

import numpy as np

import concourse.bass as bass
from concourse import mybir

F32 = mybir.dt.float32
F32R = mybir.dt.float32r
BF16 = mybir.dt.bfloat16
ALU = mybir.AluOpType
ACT = mybir.ActivationFunctionType
AX_X = mybir.AxisListType.X

P = 128
SEQ = 256
D_MODEL = 1024
D_INNER = 2048
HEAD_DIM = 128
POOL_WINDOWS = (2, 4, 8, 16)
ROPE_THETA = 10000.0
EPS = 1e-6

TT = SEQ // P
KD = D_MODEL // P
KI = D_INNER // P
COLS = 512
GK = 4
GROUPS = D_INNER // COLS
HPG = COLS // HEAD_DIM
RING = 4
EDGE = max(POOL_WINDOWS)
BAND = P + EDGE
POOL_COLS = BAND + EDGE
WARM_UP = 8
MASKED = -1e30
NO_MAX = -3.4e38

N_POOL = 4 * GROUPS
N_OUT0 = N_POOL + GROUPS
N_L1 = N_OUT0 + 2 * (KI // GK)
N_OUT1 = N_L1 + 8 * GROUPS
N_END = N_OUT1 + 8
OUT1_ORDER = [(0, 0), (0, 1), (0, 2), (1, 0), (1, 1), (1, 2), (0, 3), (1, 3)]

C_COS = 0
C_SIN = C_COS + TT * HEAD_DIM
C_END = C_SIN + TT * HEAD_DIM


def constant_tables():
    s, t = np.arange(P)[:, None], np.arange(BAND)[None, :]
    pool = np.zeros((P, GROUPS, POOL_COLS), np.float32)
    later = np.zeros((P, GROUPS, P), np.float32)
    for g, w in enumerate(POOL_WINDOWS):
        inside = ((t - s >= 0) & (t - s < w)).astype(np.float32)
        own = (t == s).astype(np.float32)
        pool[:, g, :BAND] = inside / np.float32(w) - own
        later[:, g] = pool[:, g, :P]
        count = np.minimum(np.arange(EDGE) + 1, w).astype(np.float32)
        pool[:, g, :EDGE] = inside[:, :EDGE] / count - own[:, :EDGE]
    inv = np.float32(ROPE_THETA) ** (-np.arange(0, HEAD_DIM, 2, dtype=np.float32) / np.float32(HEAD_DIM))
    ang = np.arange(SEQ, dtype=np.float32)[:, None] * inv[None, :].astype(np.float32)
    cos, sin = np.cos(ang), np.sin(ang)
    cos2 = np.concatenate([cos, cos], 1).reshape(TT, P, HEAD_DIM).transpose(1, 0, 2)
    sin2 = np.concatenate([-sin, sin], 1).reshape(TT, P, HEAD_DIM).transpose(1, 0, 2)
    table = np.concatenate([cos2.reshape(P, -1), sin2.reshape(P, -1)], 1).astype(np.float32)
    assert table.shape[1] == C_END
    return table, pool.reshape(P, -1), later.reshape(P, -1)


class Chain:

    def __init__(self, eng, sem):
        self.eng, self.sem, self.base, self.made = eng, sem, 0, 0

    def mark(self, ins):
        ins.then_inc(self.sem, 1)
        self.made += 1
        return self.base + self.made

    def wait(self, value):
        self.eng.wait_ge(self.sem, value)

    def done(self, ins):
        self.wait(self.mark(ins))

    def rebase(self, base):
        self.base, self.made = base, 0


def bass_hybrid_trunk(nc, x, w_in0, w_pool0, w_out0, w_in1, w_out1, gain_rows, qk_gains, table, pool_table, later_table, out):
    with ExitStack() as ctx:
        def sb(name, shape, dt=F32):
            return ctx.enter_context(nc.sbuf_tensor(name, shape, dt))

        def sem(name):
            return ctx.enter_context(nc.semaphore(name))

        raw = sb("raw", [P, RING, GK * COLS])
        w_hi = sb("w_hi", [P, RING, GK * COLS], F32R)
        w_lo = sb("w_lo", [P, RING, GK * COLS], F32R)
        xs = sb("xs", [P, TT, D_MODEL])
        hT_hi = sb("hT_hi", [P, KD, SEQ], F32R)
        hT_lo = sb("hT_lo", [P, KD, SEQ], F32R)
        aT_hi = sb("aT_hi", [P, KI, SEQ], F32R)
        aT_lo = sb("aT_lo", [P, KI, SEQ], F32R)
        wide = sb("wide", [P, TT, D_INNER])
        u_hi = sb("u_hi", [P, TT, COLS], F32R)
        u_lo = sb("u_lo", [P, TT, COLS], F32R)
        pool_mat = sb("pool_mat", [P, POOL_COLS], F32R)
        later_mat = sb("later_mat", [P, P], F32R)
        edge_hi = sb("edge_hi", [P, GROUPS, EDGE], F32R)
        ysb = sb("ysb", [P, 2, TT, COLS])
        k_s = sb("k_s", [P, TT, COLS])
        qT = sb("qT", [P, HPG, SEQ])
        kT = sb("kT", [P, HPG, SEQ])
        probs = sb("probs", [P, 3 * P])
        probsT = sb("probsT", [P, 3 * P])
        rope_tab = sb("rope_tab", [P, 4, TT, HEAD_DIM])
        ident = sb("ident", [P, P])
        mask = sb("mask", [P, 2 * P])
        vec_rows = qT[0:32, 0, 0:P]
        gains = sb("gains", [P, 2 * KD + KI])
        sumsq = sb("sumsq", [P, TT, 2])
        mean = sb("mean", [P, TT])
        rstd = sb("rstd", [P, TT])
        rstd_half = sb("rstd_half", [P, TT])
        minus_half = sb("minus_half", [P, 8])
        head_eps = sb("head_eps", [P, TT, HPG])
        head_root = sb("head_root", [P, TT, HPG])
        qk_sum = sb("qk_sum", [P, 2, TT, HPG])
        qk_mean = sb("qk_mean", [P, 2, TT, HPG])
        qk_rstd = sb("qk_rstd", [P, 2, TT, HPG])
        row_max = sb("row_max", [P, HPG, TT])
        exp_bias = sb("exp_bias", [P, HPG, TT])
        minus_scale = sb("minus_scale", [P, HPG, TT])
        row_sum = sb("row_sum", [P, HPG, TT])
        row_inv = sb("row_inv", [P, HPG, TT])
        o_scale = sb("o_scale", [P, HPG, TT])

        pool_mats = k_s[:, :, :].rearrange("p t n -> p (t n)")[:, 0:GROUPS * POOL_COLS].rearrange(
            "p (g n) -> p g n", g=GROUPS)
        later_mats = qT[:, :, :].rearrange("p h s -> p (h s)")[:, SEQ:SEQ + GROUPS * P].rearrange(
            "p (g n) -> p g n", g=GROUPS)

        zeros = ysb[:, 1, 0, 0:P]
        gate1 = wide[:, :, 0:COLS]
        scratch = [wide[:, :, COLS:2 * COLS], wide[:, :, 2 * COLS:3 * COLS]]
        qk = [wide[:, :, 3 * COLS:4 * COLS], k_s[:, :, :]]
        y1 = ysb[:, 0]
        v_s = ysb[:, 1]
        staged = wide[:, :, :].rearrange("p t n -> p (t n)")
        gain_q = staged[:, C_END:C_END + HEAD_DIM]
        gain_k = staged[:, C_END + HEAD_DIM:C_END + 2 * HEAD_DIM]

        acc = [[ctx.enter_context(nc.psum_tensor(f"acc{b}{t}", [P, COLS], F32)) for t in range(TT)] for b in range(2)]
        aux = [ctx.enter_context(nc.psum_tensor(f"aux{i}", [P, COLS], F32)) for i in range(4)]

        zeros_made = sem("zeros_made")
        raw_landed = [sem(f"raw_landed{i}") for i in range(RING)]
        ident_made, gains_landed = sem("ident_made"), sem("gains_landed")
        pool_landed, table_landed = sem("pool_landed"), sem("table_landed")
        x_landed = [sem(f"x_landed{h}") for h in range(2)]
        piece_landed = [[sem(f"piece_landed{n}{k}") for k in range(GK - 1)] for n in range(2)]
        piece_hi, piece_split = sem("piece_hi"), sem("piece_split")
        half_hi = [sem("half_hi0"), sem("half_hi1")]
        half_split = sem("half_split")
        hi_made = sem("hi_made")
        w_split = sem("w_split")
        w_used = sem("w_used")
        tile0_ready = sem("tile0_ready")
        gains_turned, gains_made = sem("gains_turned"), sem("gains_made")
        tables_made, poolmat_made, poolmat_placed = sem("tables_made"), sem("poolmat_made"), sem("poolmat_placed")
        sumsq_made, rstd_made = sem("sumsq_made"), sem("rstd_made")
        h_turned, h_hi, h_split = sem("h_turned"), sem("h_hi"), sem("h_split")
        u_hi_made, u_split = sem("u_hi_made"), sem("u_split")
        pooled, pooled_hi, pooled_split = sem("pooled"), sem("pooled_hi"), sem("pooled_split")
        tanh_made, gate_made = sem("tanh_made"), sem("gate_made")
        y0_made = sem("y0_made")
        y_turned, y_hi, y_split = sem("y_turned"), sem("y_hi"), sem("y_split")
        x1_made = sem("x1_made")
        qkv_out = [sem("q_out"), sem("k_out"), sem("v_out")]
        squared = [sem("q_squared"), sem("k_squared")]
        summed = [sem("q_summed"), sem("k_summed")]
        qk_scaled = sem("qk_scaled")
        rope_parts = [sem("q_rope_parts"), sem("k_rope_parts")]
        roped = [sem("q_roped"), sem("k_roped")]
        qk_turned = [sem("q_turned"), sem("k_turned")]
        qkT_made = [sem("qT_made"), sem("kT_made")]
        scores_ready, bias_made, exp_made = sem("scores_ready"), sem("bias_made"), sem("exp_made")
        p_turned, pT_made, o_ready, y1_made = sem("p_turned"), sem("pT_made"), sem("o_ready"), sem("y1_made")
        out_made, out_stored = sem("out_made"), sem("out_stored")
        dve_chain, pool_chain, act_chain = sem("dve_chain"), sem("pool_chain"), sem("act_chain")

        block = ctx.enter_context(nc.Block())

        def product_ready(eng, t, i, n):
            if t == 0:
                eng.wait_ge(tile0_ready, i + 1)
            else:
                eng.wait_ge(w_used, n + 1)

        w_in0_v = w_in0.rearrange("(k p) n -> p k n", p=P)
        w_out0_v = w_out0.rearrange("(k p) n -> p k n", p=P)
        w_in1_v = w_in1.rearrange("(k p) n -> p k n", p=P)
        w_out1_v = w_out1.rearrange("(k p) n -> p k n", p=P)

        @block.sync
        def _(sp):
            def load(slot, src, n=None):
                if n is not None:
                    sp.wait_ge(w_split, n - RING + 1)
                sp.dma_start(raw[:, slot, :].rearrange("p (k n) -> p k n", k=GK), src).then_inc(raw_landed[slot], 16)

            def load_in0(j, g, n=None):
                src = w_in0_v[:, (j % 2) * GK:(j % 2 + 1) * GK, bass.ds((j // 2) * D_INNER + g * COLS, COLS)]
                load(j, src, n)

            for n in range(2):
                c = slice(n * COLS, (n + 1) * COLS)
                sp.dma_start(xs[:, :, c], x[0].rearrange("(t p) n -> p t n", p=P)[:, :, c]).then_inc(x_landed[n], 16)
                for k in range(GK):
                    sp.dma_start(raw[:, n, k * COLS:(k + 1) * COLS],
                                 w_in0_v[:, n * GK + k, 0:COLS]).then_inc((*piece_landed[n], raw_landed[n])[k], 16)
            load_in0(2, 0)
            load_in0(3, 0)
            sp.dma_start(pool_mats.rearrange("p g n -> p (g n)"), pool_table).then_inc(pool_landed, 16)
            sp.dma_start(later_mats.rearrange("p g n -> p (g n)"), later_table).then_inc(pool_landed, 16)
            sp.dma_start(staged[:, 0:C_END], table).then_inc(table_landed, 16)
            sp.dma_start(staged[:, C_END:C_END + 2 * HEAD_DIM],
                         qk_gains.partition_broadcast(P)).then_inc(table_landed, 16)
            with sp.Fori(1, GROUPS) as g:
                for j in range(4):
                    load_in0(j, g, 4 * g + j)
            for g in range(GROUPS):
                load(g, w_pool0[g].rearrange("(k p) n -> p k n", p=P), N_POOL + g)
            for h in range(2):
                for q in range(4):
                    load(q, w_out0_v[:, q * GK:(q + 1) * GK, h * COLS:(h + 1) * COLS], N_OUT0 + 4 * h + q)
            with sp.Fori(0, GROUPS) as g:
                for j in range(8):
                    src = w_in1_v[:, (j % 2) * GK:(j % 2 + 1) * GK, bass.ds((j // 2) * D_INNER + g * COLS, COLS)]
                    load(j % RING, src, N_L1 + 8 * g + j)
            for i, (h, q) in enumerate(OUT1_ORDER):
                load(i % RING, w_out1_v[:, q * GK:(q + 1) * GK, h * COLS:(h + 1) * COLS], N_OUT1 + i)
            for i in range(2 * TT):
                h, t = i // TT, i % TT
                sp.wait_ge(out_made, i + 1)
                sp.dma_start(out[0, t * P:(t + 1) * P, h * COLS:(h + 1) * COLS],
                             ysb[:, h, t, :]).then_inc(out_stored, 16)
            sp.wait_ge(out_stored, 16 * 2 * TT)

        @block.gpsimd
        def _(pool):
            chain = Chain(pool, pool_chain)
            chain.done(pool.memset(ident[:, :], 0.0))
            pool.affine_select(out=ident[:, :], in_=ident[:, :], compare_op=ALU.not_equal, fill=1.0, base=0,
                               pattern=[[-1, P]], channel_multiplier=1).then_inc(ident_made, 1)
            chain.done(pool.memset(minus_half[:, :], -0.5))
            chain.done(pool.memset(head_eps[:, :, :], HEAD_DIM * EPS))
            chain.done(pool.memset(head_root[:, :, :], HEAD_DIM ** 0.5))
            for n in range(2):
                for k in range(GK):
                    piece = slice(k * COLS, (k + 1) * COLS)
                    pool.wait_ge((*piece_landed[n], raw_landed[n])[k], 16)
                    pool.tensor_scalar(w_hi[:, n, piece], raw[:, n, piece], 1.0, 1.0, ALU.mult,
                                       ALU.mult).then_inc(piece_hi, 1)

            def row_norm(times):
                pool.wait_ge(sumsq_made, 2 * TT * times)
                chain.done(pool.tensor_tensor(mean[:, :], sumsq[:, :, 0], sumsq[:, :, 1], ALU.add))
                chain.done(pool.tensor_scalar(mean[:, :], mean[:, :], 1.0 / D_MODEL, EPS, ALU.mult, ALU.add))
                chain.done(pool.tensor_tensor(rstd[:, :], mean[:, :], minus_half[:, 0:TT], ALU.pow))
                pool.tensor_scalar(rstd_half[:, :], rstd[:, :], 0.5, 1.0, ALU.mult, ALU.mult).then_inc(rstd_made, 1)

            row_norm(1)
            pool.wait_ge(raw_landed[2], 16)
            pool.tensor_scalar(w_hi[:, 2, 0:2 * COLS], raw[:, 2, 0:2 * COLS], 1.0, 1.0, ALU.mult,
                               ALU.mult).then_inc(half_hi[0], 1)
            chain.done(pool.memset(mask[:, :], 0.0))
            chain.done(pool.affine_select(out=mask[:, P:], in_=mask[:, P:], compare_op=ALU.is_ge, fill=MASKED,
                                          base=0, pattern=[[-1, P]], channel_multiplier=1))
            pool.wait_ge(pool_landed, 2 * 16)
            edge = pool_mats[:, :, 0:EDGE]
            chain.done(pool.tensor_scalar(edge_hi[:, :, :], edge, 1.0, 1.0, ALU.mult, ALU.mult))
            pool.tensor_tensor(pool_mats[:, :, BAND:], edge, edge_hi[:, :, :].bitcast(F32),
                               ALU.subtract).then_inc(poolmat_made, 1)
            pool.wait_ge(table_landed, 2 * 16)
            half = HEAD_DIM // 2
            for i, gain in enumerate((gain_q, gain_k)):
                for t in range(TT):
                    cos = staged[:, C_COS + t * HEAD_DIM:C_COS + (t + 1) * HEAD_DIM]
                    sin = staged[:, C_SIN + t * HEAD_DIM:C_SIN + (t + 1) * HEAD_DIM]
                    pool.tensor_tensor(rope_tab[:, 2 * i, t, :], cos, gain, ALU.mult)
                    pool.tensor_tensor(rope_tab[:, 2 * i + 1, t, 0:half], sin[:, 0:half], gain[:, half:], ALU.mult)
                    last = pool.tensor_tensor(rope_tab[:, 2 * i + 1, t, half:], sin[:, half:], gain[:, 0:half],
                                              ALU.mult)
            last.then_inc(tables_made, 1)
            row_norm(2)

            def norm_rope(g, i, first=False):
                v = qk[i]
                pool.wait_ge(qkv_out[i], TT * (g + 1))
                pool.tensor_tensor(scratch[i], v, v, ALU.mult).then_inc(squared[i], 1)
                pool.wait_ge(summed[i], g + 1)
                chain.done(pool.tensor_tensor(qk_mean[:, i], qk_sum[:, i], head_eps[:, :, :], ALU.add))
                if i == 0 and not first:
                    pool.wait_ge(exp_made, HPG * g)
                scaled = pool.tensor_tensor(qk_rstd[:, i], qk_mean[:, i],
                                            minus_half[:, :].rearrange("p (t h) -> p t h", t=TT), ALU.pow)
                if i == 0:
                    scaled.then_inc(qk_scaled, 1)
                else:
                    chain.done(scaled)
                    chain.done(pool.tensor_tensor(qk_rstd[:, i], qk_rstd[:, i], head_root[:, :, :], ALU.mult))
                v4 = v.rearrange("p t (h d) -> p t h d", h=HPG)
                s4 = scratch[i].rearrange("p t (h d) -> p t h d", h=HPG)
                if i == 1:
                    for t in range(TT):
                        ins = pool.tensor_tensor(v4[:, t], v4[:, t],
                                                 qk_rstd[:, i, t, :].unsqueeze(2).to_broadcast([P, HPG, HEAD_DIM]),
                                                 ALU.mult)
                    chain.done(ins)
                for t in range(TT):
                    for a, b in ((0, half), (half, 0)):
                        tab = rope_tab[:, 2 * i + 1, t, a:a + half].unsqueeze(1).to_broadcast([P, HPG, half])
                        ins = pool.tensor_tensor(s4[:, t, :, a:a + half], v4[:, t, :, b:b + half], tab, ALU.mult)
                chain.done(ins)
                for t in range(TT):
                    tab = rope_tab[:, 2 * i, t, :].unsqueeze(1).to_broadcast([P, HPG, HEAD_DIM])
                    ins = pool.tensor_tensor(v4[:, t], v4[:, t], tab, ALU.mult)
                ins.then_inc(rope_parts[i], 1)

            start, per_group = chain.made, 7
            norm_rope(0, 0, first=True)
            norm_rope(0, 1, first=True)
            with pool.Fori(1, GROUPS) as g:
                chain.rebase(start + per_group * g)
                norm_rope(g, 0)
                norm_rope(g, 1)
                assert chain.made == per_group, chain.made

        @block.scalar
        def _(act):
            act.dma_start(vec_rows, gain_rows).then_inc(gains_landed, 16)
            act.wait_ge(pool_chain, 2)
            act.activation(row_sum[:, 0, 0:1], minus_half[:, 0:1], ACT.Exp)

            def weight_hi(n, slot, landed):
                act.wait_ge(raw_landed[slot], landed)
                act.wait_ge(w_used, n - RING + 1)
                act.activation(w_hi[:, slot, :], raw[:, slot, :], ACT.Copy).then_inc(hi_made, 1)

            def static_hi(n):
                weight_hi(n, n % RING, 16 * (n // RING + 1))

            def turned_hi(dst, f0, bank, turned, made, gain=None):
                act.wait_ge(turned[0], turned[1])
                if gain is None:
                    act.activation(dst[:, bass.ds(f0, 2), :].rearrange("p f s -> p (f s)"), aux[bank][:, :],
                                   ACT.Copy).then_inc(made, 1)
                    return
                for j in range(2):
                    ins = act.activation(dst[:, f0 + j, :], aux[bank][:, j * SEQ:(j + 1) * SEQ], ACT.Copy,
                                         scale=gains[:, gain + f0 + j:gain + f0 + j + 1])
                ins.then_inc(made, 1)

            def squares(t, half):
                act.activation(ysb[:, half, t], xs[:, t, half * COLS:(half + 1) * COLS], ACT.Square,
                               accum_out=sumsq[:, t, half:half + 1]).then_inc(sumsq_made, 1)

            act.wait_ge(gains_turned, 1)
            act.activation(gains[:, :], aux[3][:, 0:2 * KD + KI], ACT.Copy).then_inc(gains_made, 1)
            act.wait_ge(gains_made, 1)
            for half in range(2):
                for b in (2 * half, 2 * half + 1):
                    turned_hi(hT_hi, 2 * b, b, (h_turned, b + 1), h_hi, gain=0)
                for t in range(TT):
                    act.wait_ge(x_landed[half], 16)
                    squares(t, half)
            act.wait_ge(raw_landed[2], 16)
            act.activation(w_hi[:, 2, 2 * COLS:], raw[:, 2, 2 * COLS:], ACT.Copy).then_inc(half_hi[1], 1)

            def place_pool_mat(g):
                act.wait_ge(poolmat_made, 1)
                product_ready(act, 0, 2 * g, 4 * g + 1)
                act.activation(pool_mat[:, :], pool_mats[:, g, :], ACT.Copy)
                act.activation(later_mat[:, :], later_mats[:, g, :], ACT.Copy).then_inc(poolmat_placed, 1)

            def u_upper(g):
                act.wait_ge(rstd_made, 1)
                for t in range(TT):
                    product_ready(act, t, 2 * g, 4 * g + 1)
                    act.activation(u_hi[:, t, :], acc[0][t][:, :], ACT.Copy,
                                   scale=rstd[:, t:t + 1]).then_inc(u_hi_made, 1)

            def layer0(g, first):
                if first:
                    u_upper(g)
                    act.wait_ge(raw_landed[3], 16)
                    act.activation(w_hi[:, 3, :], raw[:, 3, :], ACT.Copy).then_inc(hi_made, 1)
                    place_pool_mat(g)
                    weight_hi(4, 0, 16 * 2)
                else:
                    weight_hi(4 * g + 4, 0, 16 * (g + 2))
                    place_pool_mat(g)
                    u_upper(g)
                weight_hi(4 * g + 5, 1, 16 * (g + 2))
                for b in range(2):
                    turned_hi(aT_hi, HPG * g + 2 * b, b, (pooled, 2 * g + b + 1), pooled_hi)
                weight_hi(4 * g + 6, 2, 16 * (g + 2))
                act.wait_ge(tables_made, 1)
                for t in range(TT):
                    product_ready(act, t, 2 * g + 1, 4 * g + 3)
                    act.activation(wide[:, t, bass.ds(g * COLS, COLS)], acc[1][t][:, :], ACT.Tanh,
                                   scale=rstd_half[:, t:t + 1]).then_inc(tanh_made, 1)
                weight_hi(4 * g + 7, 3, 16 * (g + 2))

            layer0(0, first=True)
            with act.Fori(1, GROUPS) as g:
                layer0(g, first=False)

            def y0_hi(g):
                for b in range(2):
                    turned_hi(aT_hi, HPG * g + 2 * b, 2 * (g % 2) + b, (y_turned, 2 * g + b + 1), y_hi, gain=2 * KD)

            for g in range(GROUPS):
                if g > 0:
                    static_hi(N_POOL + 3 + g)
                    y0_hi(g - 1)
            static_hi(N_OUT0 + 3)
            y0_hi(GROUPS - 1)

            def h1_hi(half):
                for t in range(TT):
                    act.wait_ge(x1_made, TT * half + t + 1)
                    if half == 0 and t == 0:
                        act.wait_ge(rstd_made, 1)
                    squares(t, half)
                for b in range(2):
                    turned_hi(hT_hi, 4 * half + 2 * b, 2 * half + b, (h_turned, 4 + 2 * half + b + 1), h_hi, gain=KD)

            for n in range(N_OUT0 + 4, N_OUT0 + 8):
                static_hi(n)
            h1_hi(0)
            for n in range(N_OUT0 + 8, N_L1 + 3):
                static_hi(n)

            def exp_scores(g, h):
                act.wait_ge(bias_made, HPG * g + h + 1)
                if h > 0:
                    act.wait_ge(p_turned, HPG * g + h)
                act.activation(probs[:, 0:P], aux[h % 2][:, 0:P], ACT.Exp, bias=exp_bias[:, h, 0:1],
                               scale=qk_rstd[:, 0, 0, h:h + 1], accum_out=row_sum[:, h, 0:1])
                act.activation(probs[:, P:3 * P], aux[h % 2][:, P:3 * P], ACT.Exp, bias=exp_bias[:, h, 1:2],
                               scale=qk_rstd[:, 0, 1, h:h + 1], accum_out=row_sum[:, h, 1:2]).then_inc(exp_made, 1)

            def probs_out(g, h):
                act.wait_ge(p_turned, HPG * g + h + 1)
                if h > 0:
                    act.wait_ge(o_ready, HPG * g + h)
                act.activation(probsT[:, :], aux[2][:, 0:3 * P], ACT.Copy).then_inc(pT_made, 1)

            def qkv_evacuate(g, which, first=False):
                if first:
                    pass
                elif which < 2:
                    act.wait_ge(qk_turned[which], 2 * g)
                else:
                    act.wait_ge(o_ready, HPG * g)
                dst = (*qk, v_s)[which]
                for t in range(TT):
                    product_ready(act, t, 14 + 4 * g + which, N_L1 + 8 * g + 2 * which + 1)
                    ins = act.activation(dst[:, t, :], acc[which % 2][t][:, :], ACT.Copy, scale=rstd[:, t:t + 1])
                    ins.then_inc(qkv_out[which], 1)

            def qkT_out(g, i):
                for b in range(2):
                    act.wait_ge(qk_turned[i], 2 * g + b + 1)
                    dst = (qT, kT)[i]
                    act.activation(dst[:, 2 * b:2 * b + 2, :].rearrange("p h s -> p (h s)"), aux[2 * i + b][:, :],
                                   ACT.Copy).then_inc(qkT_made[i], 1)

            def tanh_z(g, first):
                for t in range(TT):
                    product_ready(act, t, 17 + 4 * g, N_L1 + 8 * g + 7)
                    if not first:
                        act.wait_ge(y1_made, HPG * g)
                    act.activation(gate1[:, t, :], acc[1][t][:, :], ACT.Tanh,
                                   scale=rstd_half[:, t:t + 1]).then_inc(tanh_made, 1)

            def y1_hi(g):
                for b in range(2):
                    turned_hi(aT_hi, HPG * g + 2 * b, b, (y_turned, 8 + 2 * g + b + 1), y_hi)

            def layer1(g, attend):
                def w(j):
                    weight_hi(N_L1 + 3 + 8 * g + j, (N_L1 + 3 + j) % RING, 16 * ((N_L1 + 3 + j) // RING + 1) + 32 * g)
                w(0)
                if attend:
                    exp_scores(g - 1, 0)
                qkv_evacuate(g, 0, not attend)
                w(1)
                if attend:
                    exp_scores(g - 1, 1)
                    probs_out(g - 1, 0)
                w(2)
                if attend:
                    exp_scores(g - 1, 2)
                    probs_out(g - 1, 1)
                qkv_evacuate(g, 1, not attend)
                w(3)
                if attend:
                    exp_scores(g - 1, 3)
                    probs_out(g - 1, 2)
                w(4)
                if attend:
                    probs_out(g - 1, 3)
                w(5)
                qkv_evacuate(g, 2, not attend)
                w(6)
                qkT_out(g, 0)
                w(7)
                tanh_z(g, not attend)
                if attend:
                    y1_hi(g - 1)
                qkT_out(g, 1)

            h1_hi(1)
            act.wait_ge(rstd_made, 2)
            layer1(0, attend=False)
            with act.Fori(1, GROUPS) as g:
                layer1(g, attend=True)

            last = GROUPS - 1
            for n in range(N_OUT1 + 3, N_END):
                static_hi(n)
                j = n - N_OUT1 - 3
                if j < HPG:
                    exp_scores(last, j)
                if 1 <= j <= HPG:
                    probs_out(last, j - 1)
            y1_hi(last)

        @block.tensor
        def _(pe):
            def granule(n, slot, buf, free, src_hi, src_lo, k0, first, last, need=None, mid=None, mid_at=2,
                        halves=False):
                if first and free:
                    pe.wait_ge(*free)
                if halves:
                    pe.wait_ge(half_split, 1)
                else:
                    pe.wait_ge(w_split, n + 1)
                order = [(t, k) for t in range(TT) for k in range(GK)] if last and not mid and not need else \
                    [(t, k) for k in range(GK) for t in range(TT)]
                for i, (t, k) in enumerate(order):
                    if mid and i == mid_at * TT:
                        mid()
                    if halves and i == GK // 2 * TT:
                        pe.wait_ge(w_split, n + 1)
                    if need and t == 0:
                        need(k0 + k)
                    whi = w_hi[:, slot, k * COLS:(k + 1) * COLS]
                    wlo = w_lo[:, slot, k * COLS:(k + 1) * COLS]
                    shi = src_hi[:, k0 + k, t * P:(t + 1) * P]
                    slo = src_lo[:, k0 + k, t * P:(t + 1) * P]
                    a = acc[buf][t][:, :]
                    pe.matmul(a, shi, whi, start=first and k == 0, stop=False)
                    pe.matmul(a, shi, wlo, start=False, stop=False)
                    ins = pe.matmul(a, slo, whi, start=False, stop=last and k == GK - 1)
                    if last and k == GK - 1 and t == 0:
                        ins.then_inc(tile0_ready, 1)
                    if i == TT * GK - 1:
                        ins.then_inc(w_used, 1)

            def early_granule(n, mid=None):
                for i in range(3):
                    if mid and i == 2:
                        mid()
                    for t, k in [(t, k) for k in range(GK) for t in range(TT)] if i < 2 else \
                            [(t, k) for t in range(TT) for k in range(GK)]:
                        if t == 0 and i == 0:
                            pe.wait_ge(h_hi, 2 * n + k // 2 + 1)
                            pe.wait_ge(piece_hi, GK * n + k + 1)
                        if t == 0 and i == 1:
                            pe.wait_ge(*((piece_split, (GK - 1) * n + k + 1) if k < GK - 1 else (w_split, n + 1)))
                        if t == 0 and i == 2:
                            pe.wait_ge(h_split, 2 * n + k // 2 + 1)
                        src, w = (hT_lo if i == 2 else hT_hi), (w_lo if i == 1 else w_hi)
                        ins = pe.matmul(acc[0][t][:, :], src[:, GK * n + k, t * P:(t + 1) * P],
                                        w[:, n, k * COLS:(k + 1) * COLS], start=(n, i, k) == (0, 0, 0),
                                        stop=(n, i, k) == (1, 2, GK - 1))
                        if n == 1 and i == 2 and k == GK - 1 and t == 0:
                            ins.then_inc(tile0_ready, 1)
                ins.then_inc(w_used, 1)

            def turn(dst_banks, src, made, tiles=range(HPG)):
                for f in tiles:
                    for t in range(TT):
                        c = (f % 2) * SEQ + t * P
                        ins = pe.transpose(aux[dst_banks[f // 2]][:, c:c + P], src[:, t, f * P:(f + 1) * P],
                                           ident[:, :])
                    if f % 2:
                        ins.then_inc(made, 1)

            pe.wait_ge(zeros_made, 1)
            for _ in range(WARM_UP):
                pe.matmul(acc[1][1][:, 0:P], zeros, zeros, start=True, stop=True)

            pe.wait_ge(ident_made, 1)
            pe.wait_ge(gains_landed, 16)
            pe.transpose(aux[3][:, 0:32], vec_rows, ident[0:32, 0:32]).then_inc(gains_turned, 1)
            pe.wait_ge(x_landed[0], 16)
            turn((0, 1), xs[:, :, 0:COLS], h_turned)

            def turn_x_rest():
                pe.wait_ge(x_landed[1], 16)
                pe.wait_ge(gains_made, 1)
                turn((2, 3), xs[:, :, COLS:], h_turned)

            early_granule(0, mid=turn_x_rest)
            early_granule(1)

            def h_needed(base):
                def need(k):
                    if k % 2 == 0:
                        pe.wait_ge(h_split, base + k // 2 + 1)
                return need

            def pool_tokens(g):
                pe.wait_ge(poolmat_placed, g + 1)
                pe.wait_ge(u_split, TT * (g + 1))
                for f in range(HPG):
                    bank, c = aux[f // 2], (f % 2) * SEQ
                    for t in range(TT):
                        hi, lo = (part[:, t, f * P:(f + 1) * P] for part in (u_hi, u_lo))
                        if t == 0:
                            out0 = bank[:, c:c + BAND]
                            pe.matmul(out0, hi, pool_mat[:, 0:BAND], start=True, stop=False, skip_group_check=True)
                            pe.matmul(bank[:, c:c + EDGE], hi, pool_mat[:, BAND:], start=False, stop=False,
                                      skip_group_check=True)
                            pe.matmul(out0, lo, pool_mat[:, 0:BAND], start=False, stop=False, skip_group_check=True)
                        else:
                            out1 = bank[:, c + P:c + 2 * P]
                            pe.matmul(out1, hi, later_mat[:, :], start=False, stop=False, skip_group_check=True)
                            ins = pe.matmul(out1, lo, later_mat[:, :], start=False, stop=True, skip_group_check=True)
                    if f % 2:
                        ins.then_inc(pooled, 1)

            def layer0(g, first):
                for j in range(2 if first else 0, 4):
                    granule(4 * g + j, j, j // 2, None, hT_hi, hT_lo, GK * (j % 2), first=j % 2 == 0, last=j % 2 == 1,
                            halves=first and j == 2)
                    if j == 2:
                        pool_tokens(g)

            layer0(0, first=True)
            with pe.Fori(1, GROUPS) as g:
                layer0(g, first=False)

            def turn_y0(g):
                pe.wait_ge(y0_made, g + 1)
                if g >= 2:
                    pe.wait_ge(y_split, 2 * (g - 1))
                turn((2 * (g % 2), 2 * (g % 2) + 1), ysb[:, g % 2], y_turned)

            pe.wait_ge(pooled_split, 2 * GROUPS)
            for g in range(GROUPS):
                free = (y0_made, g - 1) if g >= 2 else ((u_split, gate_made)[g], TT * GROUPS)
                granule(N_POOL + g, g, g % 2, free, aT_hi, aT_lo, HPG * g, first=True, last=True)
                if g > 0:
                    turn_y0(g - 1)

            def turn_x1(half):
                pe.wait_ge(x1_made, TT * (half + 1))
                turn((2 * half, 2 * half + 1), xs[:, :, half * COLS:(half + 1) * COLS], h_turned)

            for half in range(2):
                for q in range(4):
                    pe.wait_ge(y_split, 2 * (q + 1))
                    granule(N_OUT0 + 4 * half + q, q, half, (y0_made, 3 + half), aT_hi, aT_lo, GK * q, first=q == 0, last=q == 3)
                    if (half, q) == (0, 0):
                        turn_y0(GROUPS - 1)
                    if (half, q) == (1, 0):
                        turn_x1(0)

            def scores(g, h):
                for i in range(2):
                    pe.wait_ge(qkT_made[i], 2 * (g + 1))
                if h < 2:
                    pe.wait_ge(y_split, 8 + 2 * g)
                else:
                    pe.wait_ge(exp_made, HPG * g + h - 1)
                s = aux[h % 2]
                pe.matmul(s[:, 0:P], qT[:, h, 0:P], kT[:, h, 0:P], start=True, stop=True)
                pe.matmul(s[:, P:3 * P], qT[:, h, P:SEQ], kT[:, h, :], start=True, stop=True).then_inc(scores_ready, 1)

            def turn_probs(g, h):
                pe.wait_ge(exp_made, HPG * g + h + 1)
                if h > 0:
                    pe.wait_ge(pT_made, HPG * g + h)
                for i in range(3):
                    ins = pe.transpose(aux[2][:, i * P:(i + 1) * P], probs[:, i * P:(i + 1) * P], ident[:, :])
                ins.then_inc(p_turned, 1)

            def values(g, h):
                pe.wait_ge(pT_made, HPG * g + h + 1)
                pe.wait_ge(qkv_out[2], TT * (g + 1))
                if h > 0:
                    pe.wait_ge(y1_made, HPG * g + h)
                v = [v_s[:, t, h * P:(h + 1) * P] for t in range(TT)]
                pe.matmul(aux[3][:, 0:P], probsT[:, 0:P], v[0], start=True, stop=True)
                pe.matmul(aux[3][:, P:2 * P], probsT[:, P:2 * P], v[0], start=True, stop=False)
                pe.matmul(aux[3][:, P:2 * P], probsT[:, 2 * P:3 * P], v[1], start=False,
                          stop=True).then_inc(o_ready, 1)

            def turn_qk(g, i, first):
                pe.wait_ge(roped[i], g + 1)
                if first:
                    pass
                elif i == 0:
                    pe.wait_ge(exp_made, HPG * g)
                else:
                    pe.wait_ge(y1_made, HPG * g)
                turn((2 * i, 2 * i + 1), qk[i], qk_turned[i])

            def turn_y1(g, after_q):
                pe.wait_ge(y1_made, HPG * (g + 1))
                if after_q is not None:
                    pe.wait_ge(qkT_made[0], 2 * (after_q + 1))
                turn((0, 1), y1, y_turned)

            def attend(g, j):
                if j < HPG:
                    scores(g, j)
                if 2 <= j < HPG + 2:
                    values(g, j - 2)
                if 1 <= j < HPG + 1:
                    turn_probs(g, j - 1)

            def layer1(g, first):
                for j in range(8):
                    which = j // 2
                    free = {0: (x1_made, TT) if first else (qkv_out[2], TT * g),
                            1: (x1_made, 2 * TT) if first else (gate_made, TT * (GROUPS + g)),
                            2: (qkv_out[0], TT * (g + 1)), 3: (qkv_out[1], TT * (g + 1))}[which]
                    granule(N_L1 + 8 * g + j, j % RING, which % 2, free, hT_hi, hT_lo,
                            GK * (j % 2), first=j % 2 == 0, last=j % 2 == 1,
                            need=h_needed(4) if first and j < 2 else None,
                            mid=(lambda: turn_x1(1)) if first and j == 0 else None)
                    if not first:
                        attend(g - 1, j)
                    if j == 6:
                        turn_qk(g, 0, first)
                    if j == 7:
                        if not first:
                            turn_y1(g - 1, g)
                        turn_qk(g, 1, first)

            layer1(0, first=True)
            with pe.Fori(1, GROUPS) as g:
                layer1(g, first=False)

            last = GROUPS - 1

            def turn_y1_last(b):
                pe.wait_ge(y1_made, HPG * last + 2 * b + 2)
                pe.wait_ge(exp_made, HPG * last + 3 + b)
                turn((0, 1), y1, y_turned, tiles=(2 * b, 2 * b + 1))

            def y_needed(k):
                if k % 2 == 0:
                    pe.wait_ge(y_split, 8 + k // 2 + 1)

            for j, (half, q) in enumerate(OUT1_ORDER):
                granule(N_OUT1 + j, j % RING, half, ((qkv_out[2], TT * GROUPS), (gate_made, 2 * TT * GROUPS))[half],
                        aT_hi, aT_lo, GK * q, first=q == 0, last=q == 3, need=y_needed if j < 7 else None,
                        mid=(lambda: turn_y1_last(1)) if j == 6 else None, mid_at=1)
                attend(last, j)
                if j == 4:
                    turn_y1_last(0)

        @block.vector
        def _(dve):
            chain = Chain(dve, dve_chain)
            dve.memset(zeros, 0.0).then_inc(zeros_made, 1)

            def weight_lo(n, slot):
                dve.wait_ge(hi_made, n - RING + 2)
                dve.tensor_tensor(w_lo[:, slot, :], raw[:, slot, :], w_hi[:, slot, :].bitcast(F32),
                                  ALU.subtract).then_inc(w_split, 1)

            def turned_lo(dst, hi_src, f0, bank, hi_sem, hi_count, made, gain=None):
                dve.wait_ge(hi_sem, hi_count)
                if gain is None:
                    dve.tensor_tensor(dst[:, bass.ds(f0, 2), :].rearrange("p f s -> p (f s)"), aux[bank][:, :],
                                      hi_src[:, bass.ds(f0, 2), :].bitcast(F32).rearrange("p f s -> p (f s)"),
                                      ALU.subtract).then_inc(made, 1)
                    return
                for j in range(2):
                    ins = dve.scalar_tensor_tensor(dst[:, f0 + j, :], aux[bank][:, j * SEQ:(j + 1) * SEQ],
                                                   gains[:, gain + f0 + j:gain + f0 + j + 1],
                                                   hi_src[:, f0 + j, :].bitcast(F32), ALU.mult, ALU.subtract)
                ins.then_inc(made, 1)

            def part_lo(n, a, b, made):
                part = slice(a * COLS, b * COLS)
                return dve.tensor_tensor(w_lo[:, n, part], raw[:, n, part], w_hi[:, n, part].bitcast(F32),
                                         ALU.subtract).then_inc(made, 1)

            def piece_lo(n, k):
                dve.wait_ge(piece_hi, GK * n + k + 1)
                part_lo(n, k, k + 1, piece_split if k < GK - 1 else w_split)

            def h0_lo(b):
                turned_lo(hT_lo, hT_hi, 2 * b, b, h_hi, b + 1, h_split, gain=0)

            for n in range(2):
                piece_lo(n, 0)
                piece_lo(n, 1)
                h0_lo(2 * n)
                piece_lo(n, 2)
                piece_lo(n, 3)
                h0_lo(2 * n + 1)
            dve.wait_ge(half_hi[0], 1)
            part_lo(2, 0, 2, half_split)
            dve.wait_ge(half_hi[1], 1)
            part_lo(2, 2, 4, w_split)

            def layer0(g, first):
                if not first:
                    weight_lo(4 * g + 4, 0)
                dve.wait_ge(rstd_made, 1)
                for t in range(TT):
                    dve.wait_ge(u_hi_made, TT * g + t + 1)
                    ins = dve.scalar_tensor_tensor(u_lo[:, t, :], acc[0][t][:, :], rstd[:, t:t + 1],
                                                   u_hi[:, t, :].bitcast(F32), ALU.mult, ALU.subtract)
                    ins.then_inc(u_split, 1)
                if first:
                    weight_lo(3, 3)
                    weight_lo(4, 0)
                weight_lo(4 * g + 5, 1)
                for b in range(2):
                    turned_lo(aT_lo, aT_hi, HPG * g + 2 * b, b, pooled_hi, 2 * g + b + 1, pooled_split)
                for t in range(TT):
                    dve.wait_ge(tanh_made, TT * g + t + 1)
                    gate = wide[:, t, bass.ds(g * COLS, COLS)]
                    ins = dve.scalar_tensor_tensor(gate, gate, 1.0, acc[1][t][:, :], ALU.add, ALU.mult)
                    ins.then_inc(gate_made, 1)
                weight_lo(4 * g + 6, 2)
                weight_lo(4 * g + 7, 3)

            layer0(0, first=True)
            with dve.Fori(1, GROUPS) as g:
                layer0(g, first=False)

            def y0_lo(g):
                for b in range(2):
                    turned_lo(aT_lo, aT_hi, HPG * g + 2 * b, 2 * (g % 2) + b, y_hi, 2 * g + b + 1, y_split,
                              gain=2 * KD)

            dve.wait_ge(gate_made, TT * GROUPS)
            for g in range(GROUPS):
                n = N_POOL + 3 + g
                if g > 0:
                    weight_lo(n, n % RING)
                for t in range(TT):
                    product_ready(dve, t, 8 + g, N_POOL + g)
                    if g >= 2:
                        dve.wait_ge(y_turned, 2 * (g - 1))
                    ins = dve.scalar_tensor_tensor(ysb[:, g % 2, t, :], acc[g % 2][t][:, :], rstd_half[:, t:t + 1],
                                                   wide[:, t, g * COLS:(g + 1) * COLS], ALU.mult, ALU.mult)
                    if t == TT - 1:
                        ins.then_inc(y0_made, 1)
                if g > 0:
                    y0_lo(g - 1)
            weight_lo(N_OUT0 + 3, (N_OUT0 + 3) % RING)
            y0_lo(GROUPS - 1)

            def x1(half):
                for t in range(TT):
                    product_ready(dve, t, 12 + half, N_OUT0 + 4 * half + 3)
                    s = xs[:, t, half * COLS:(half + 1) * COLS]
                    ins = dve.tensor_tensor(s, acc[half][t][:, :], s, ALU.add)
                    ins.then_inc(x1_made, 1)

            def h1_lo(half):
                for b in range(2):
                    turned_lo(hT_lo, hT_hi, 4 * half + 2 * b, 2 * half + b, h_hi, 4 + 2 * half + b + 1, h_split,
                              gain=KD)

            for n in range(N_OUT0 + 4, N_OUT0 + 7):
                weight_lo(n, n % RING)
            x1(0)
            weight_lo(N_OUT0 + 7, (N_OUT0 + 7) % RING)
            h1_lo(0)
            for n in range(N_OUT0 + 8, N_L1 + 3):
                weight_lo(n, n % RING)
            x1(1)

            def head_max(g, h):
                dve.wait_ge(qk_scaled, g + 1)
                dve.wait_ge(scores_ready, HPG * g + h + 1)
                dve.tensor_scalar(minus_scale[:, h, :], qk_rstd[:, 0, :, h], -1.0, 1.0, ALU.mult, ALU.mult)
                s = aux[h % 2]
                dve.tensor_tensor_reduce(s[:, 0:P], s[:, 0:P], mask[:, P:], 1.0, NO_MAX, ALU.add, ALU.max,
                                         row_max[:, h, 0:1])
                chain.done(dve.tensor_tensor_reduce(s[:, P:3 * P], s[:, P:3 * P], mask[:, :], 1.0, NO_MAX,
                                                    ALU.add, ALU.max, row_max[:, h, 1:2]))
                dve.tensor_tensor(exp_bias[:, h, :], row_max[:, h, :], minus_scale[:, h, :],
                                  ALU.mult).then_inc(bias_made, 1)

            def head_out(g, h):
                dve.wait_ge(exp_made, HPG * g + h + 1)
                chain.done(dve.reciprocal(row_inv[:, h, :], row_sum[:, h, :]))
                chain.done(dve.tensor_tensor(o_scale[:, h, :], row_inv[:, h, :], rstd_half[:, :], ALU.mult))
                dve.wait_ge(o_ready, HPG * g + h + 1)
                dve.wait_ge(y_turned, 8 + 2 * g)
                for t in range(TT):
                    ins = dve.scalar_tensor_tensor(y1[:, t, h * P:(h + 1) * P], aux[3][:, t * P:(t + 1) * P],
                                                   o_scale[:, h, t:t + 1], gate1[:, t, h * P:(h + 1) * P],
                                                   ALU.mult, ALU.mult)
                ins.then_inc(y1_made, 1)

            def sum_squares(g, i):
                dve.wait_ge(squared[i], g + 1)
                dve.tensor_reduce(qk_sum[:, i], scratch[i].rearrange("p t (h d) -> p t h d", h=HPG), AX_X,
                                  ALU.add).then_inc(summed[i], 1)

            def rope_sum(g, i):
                dve.wait_ge(rope_parts[i], g + 1)
                dve.tensor_tensor(qk[i], qk[i], scratch[i], ALU.add).then_inc(roped[i], 1)

            def gate_z(g):
                for t in range(TT):
                    dve.wait_ge(tanh_made, TT * (GROUPS + g) + t + 1)
                    ins = dve.scalar_tensor_tensor(gate1[:, t, :], gate1[:, t, :], 1.0, acc[1][t][:, :],
                                                   ALU.add, ALU.mult)
                    ins.then_inc(gate_made, 1)

            def y1_lo_bank(g, b):
                turned_lo(aT_lo, aT_hi, HPG * g + 2 * b, b, y_hi, 8 + 2 * g + b + 1, y_split)

            def y1_lo(g):
                for b in range(2):
                    y1_lo_bank(g, b)

            def layer1(g, attend):
                def w(j):
                    weight_lo(N_L1 + 3 + 8 * g + j, (N_L1 + 3 + j) % RING)
                if attend:
                    head_max(g - 1, 0)
                w(0)
                if attend:
                    head_max(g - 1, 1)
                w(1)
                if attend:
                    dve.wait_ge(gate_made, TT * (GROUPS + g))
                    head_max(g - 1, 2)
                    head_out(g - 1, 0)
                sum_squares(g, 0)
                w(2)
                if attend:
                    head_max(g - 1, 3)
                    head_out(g - 1, 1)
                w(3)
                if attend:
                    head_out(g - 1, 2)
                w(4)
                sum_squares(g, 1)
                rope_sum(g, 0)
                if attend:
                    head_out(g - 1, 3)
                w(5)
                w(6)
                rope_sum(g, 1)
                w(7)
                gate_z(g)
                if attend:
                    y1_lo(g - 1)

            h1_lo(1)
            dve.wait_ge(tables_made, 1)
            layer1(0, attend=False)
            start, per_group = chain.made, 3 * HPG
            with dve.Fori(1, GROUPS) as g:
                chain.rebase(start + per_group * (g - 1))
                layer1(g, attend=True)
                assert chain.made == per_group
            chain.rebase(start + per_group * (GROUPS - 1))

            last = GROUPS - 1
            dve.wait_ge(gate_made, TT * 2 * GROUPS)
            for j in range(6):
                if j < HPG:
                    head_max(last, j)
                if j == 5:
                    y1_lo_bank(last, 0)
                if j >= 2:
                    head_out(last, j - 2)
                n = N_OUT1 + 3 + j
                if n < N_END:
                    weight_lo(n, n % RING)
            y1_lo_bank(last, 1)
            for half in range(2):
                for t in range(TT):
                    product_ready(dve, t, 30 + half, N_OUT1 + 6 + half)
                    dve.wait_ge(y_turned, 16)
                    dve.tensor_tensor(ysb[:, half, t, :], acc[half][t][:, :], xs[:, t, half * COLS:(half + 1) * COLS],
                                      ALU.add).then_inc(out_made, 1)


_INS = ["x", "w_in0", "w_pool0", "w_out0", "w_in1", "w_out1"]


def kernel(**inputs):
    import concourse.bacc as _bacc
    from concourse import mybir as _mybir
    from concourse.bass_utils import run_bass_kernel_spmd as _run

    nc = _bacc.Bacc("TRN2", target_bir_lowering=False, num_devices=1)
    arrays, args = {}, []
    table, pool_table, later_table = constant_tables()
    gain_rows = np.concatenate([np.asarray(inputs[n]) for n in ("norm0", "norm1", "pool_scale0")]).reshape(-1, P)
    qk_gains = np.concatenate([np.asarray(inputs[n]) for n in ("q_norm1", "k_norm1")])
    laid_out = [(n, np.ascontiguousarray(inputs[n])) for n in _INS]
    laid_out += [("gain_rows", gain_rows), ("qk_gains", qk_gains), ("table", table), ("pool_table", pool_table),
                 ("later_table", later_table)]
    for name, a in laid_out:
        arrays[f"in_{name}_dram"] = a
        args.append(nc.dram_tensor(f"in_{name}_dram", a.shape, _mybir.dt.from_np(a.dtype), kind="ExternalInput").ap())
    args.append(nc.dram_tensor("out_0_dram", (1, SEQ, D_MODEL), F32, kind="ExternalOutput").ap())
    bass_hybrid_trunk(nc, *args)
    r = _run(nc, [arrays], core_ids=[0])
    return r.results[0]["out_0_dram"]
```

```python
from contextlib import ExitStack

import numpy as np

import concourse.bass as bass
from concourse import mybir

F32 = mybir.dt.float32
F32R = mybir.dt.float32r
ALU = mybir.AluOpType
ACT = mybir.ActivationFunctionType
AX_X = mybir.AxisListType.X

P = 128
SEQ = 256
D_MODEL = 1024
D_INNER = 2048
HEAD_DIM = 128
POOL_WINDOWS = (2, 4, 8, 16)
ROPE_THETA = 10000.0
EPS = 1e-6

TT = SEQ // P
KD = D_MODEL // P
KI = D_INNER // P
COLS = 512
GK = 4
GROUPS = D_INNER // COLS
HPG = COLS // HEAD_DIM
RING = 4
EDGE = max(POOL_WINDOWS)
BAND = P + EDGE
WARM_UP = 8
MASKED = -1e30
NO_MAX = -3.4e38

N_POOL = 4 * GROUPS
N_OUT0 = N_POOL + GROUPS
N_L1 = N_OUT0 + 2 * (KI // GK)
N_OUT1 = N_L1 + 8 * GROUPS
N_END = N_OUT1 + 8
OUT1_ORDER = [(0, 0), (0, 1), (0, 2), (1, 0), (1, 1), (1, 2), (0, 3), (1, 3)]

C_COS = 0
C_SIN = C_COS + TT * HEAD_DIM
C_END = C_SIN + TT * HEAD_DIM


def constant_tables():
    s, t = np.arange(P)[:, None], np.arange(BAND)[None, :]
    pool = np.zeros((P, GROUPS, BAND), np.float32)
    later = np.zeros((P, GROUPS, P), np.float32)
    for g, w in enumerate(POOL_WINDOWS):
        inside = ((t - s >= 0) & (t - s < w)).astype(np.float32)
        own = (t == s).astype(np.float32)
        pool[:, g, :BAND] = inside / np.float32(w) - own
        later[:, g] = pool[:, g, :P]
        count = np.minimum(np.arange(EDGE) + 1, w).astype(np.float32)
        pool[:, g, :EDGE] = inside[:, :EDGE] / count - own[:, :EDGE]
    inv = np.float32(ROPE_THETA) ** (-np.arange(0, HEAD_DIM, 2, dtype=np.float32) / np.float32(HEAD_DIM))
    ang = np.arange(SEQ, dtype=np.float32)[:, None] * inv[None, :].astype(np.float32)
    cos, sin = np.cos(ang), np.sin(ang)
    cos2 = np.concatenate([cos, cos], 1).reshape(TT, P, HEAD_DIM).transpose(1, 0, 2)
    sin2 = np.concatenate([-sin, sin], 1).reshape(TT, P, HEAD_DIM).transpose(1, 0, 2)
    table = np.concatenate([cos2.reshape(P, -1), sin2.reshape(P, -1)], 1).astype(np.float32)
    assert table.shape[1] == C_END
    return table, pool.reshape(P, -1), later.reshape(P, -1)


class Chain:

    def __init__(self, eng, sem):
        self.eng, self.sem, self.base, self.made = eng, sem, 0, 0

    def mark(self, ins):
        ins.then_inc(self.sem, 1)
        self.made += 1
        return self.base + self.made

    def wait(self, value):
        self.eng.wait_ge(self.sem, value)

    def done(self, ins):
        self.wait(self.mark(ins))

    def rebase(self, base):
        self.base, self.made = base, 0


def bass_hybrid_trunk(nc, x, w_in0, w_pool0, w_out0, w_in1, w_out1, xT_in, gains_in, qk_gains, table, pool_table,
                      later_table, out):
    with ExitStack() as ctx:
        def sb(name, shape, dt=F32):
            return ctx.enter_context(nc.sbuf_tensor(name, shape, dt))

        def sem(name):
            return ctx.enter_context(nc.semaphore(name))

        raw = sb("raw", [P, RING, GK * COLS])
        w_hi = sb("w_hi", [P, RING, GK * COLS], F32R)
        w_lo = sb("w_lo", [P, RING, GK * COLS], F32R)
        xs = sb("xs", [P, TT, D_MODEL])
        hT_hi = sb("hT_hi", [P, KD, SEQ], F32R)
        hT_lo = sb("hT_lo", [P, KD, SEQ], F32R)
        aT_hi = sb("aT_hi", [P, KI, SEQ], F32R)
        aT_lo = sb("aT_lo", [P, KI, SEQ], F32R)
        wide = sb("wide", [P, TT, D_INNER])
        u_s = sb("u_s", [P, TT, COLS])
        ysb = sb("ysb", [P, 2, TT, COLS])
        k_s = sb("k_s", [P, TT, COLS])
        qT = sb("qT", [P, HPG, SEQ])
        kT = sb("kT", [P, HPG, SEQ])
        probs = sb("probs", [P, 3 * P])
        probsT = sb("probsT", [P, 3 * P])
        rope_tab = sb("rope_tab", [P, 4, TT, HEAD_DIM])
        ident = sb("ident", [P, P])
        mask = sb("mask", [P, 2 * P])
        gains = sb("gains", [P, 2 * KD + KI])
        sumsq = sb("sumsq", [P, TT, 2])
        mean = sb("mean", [P, TT])
        ones = sb("ones", [P, 1])
        rstd = sb("rstd", [P, TT])
        rstd_half = sb("rstd_half", [P, TT])
        minus_half = sb("minus_half", [P, 8])
        head_eps = sb("head_eps", [P, TT, HPG])
        head_root = sb("head_root", [P, TT, HPG])
        qk_sum = sb("qk_sum", [P, 2, TT, HPG])
        qk_mean = sb("qk_mean", [P, 2, TT, HPG])
        qk_rstd = sb("qk_rstd", [P, 2, TT, HPG])
        row_max = sb("row_max", [P, HPG, TT])
        exp_bias = sb("exp_bias", [P, HPG, TT])
        minus_scale = sb("minus_scale", [P, HPG, TT])
        row_sum = sb("row_sum", [P, HPG, TT])
        row_inv = sb("row_inv", [P, HPG, TT])
        o_scale = sb("o_scale", [P, HPG, TT])

        pool_mats = k_s[:, :, :].rearrange("p t n -> p (t n)")[:, 0:GROUPS * BAND].rearrange(
            "p (g n) -> p g n", g=GROUPS)
        later_mats = qT[:, :, :].rearrange("p h s -> p (h s)")[:, SEQ:SEQ + GROUPS * P].rearrange(
            "p (g n) -> p g n", g=GROUPS)

        zeros = k_s[:, 1, COLS - P:]
        xT = wide[:, :, :].rearrange("p t n -> p (t n)")[:, 2 * D_MODEL:].rearrange("p (k s) -> p k s", k=KD)
        sqT = ysb[:, :, :, :].rearrange("p b t n -> p (b t n)")
        gate1 = wide[:, :, 0:COLS]
        scratch = [wide[:, :, COLS:2 * COLS], wide[:, :, 2 * COLS:3 * COLS]]
        qk = [wide[:, :, 3 * COLS:4 * COLS], k_s[:, :, :]]
        y1 = ysb[:, 0]
        v_s = ysb[:, 1]
        staged = wide[:, :, :].rearrange("p t n -> p (t n)")
        gain_q = staged[:, C_END:C_END + HEAD_DIM]
        gain_k = staged[:, C_END + HEAD_DIM:C_END + 2 * HEAD_DIM]

        acc = [[ctx.enter_context(nc.psum_tensor(f"acc{b}{t}", [P, COLS], F32)) for t in range(TT)] for b in range(2)]
        aux = [ctx.enter_context(nc.psum_tensor(f"aux{i}", [P, COLS], F32)) for i in range(4)]

        zeros_made = sem("zeros_made")
        raw_landed = [sem(f"raw_landed{i}") for i in range(RING)]
        ident_made, gains_landed = sem("ident_made"), sem("gains_landed")
        pool_landed, table_landed = sem("pool_landed"), sem("table_landed")
        x_landed, xT_landed = sem("x_landed"), [sem(f"xT_landed{b}") for b in range(KD // 2)]
        piece_landed = [[sem(f"piece_landed{n}{k}") for k in range(GK - 1)] for n in range(2)]
        piece_hi, piece_split = sem("piece_hi"), sem("piece_split")
        half_hi = [sem("half_hi0"), sem("half_hi1")]
        half_split = sem("half_split")
        hi_made = sem("hi_made")
        w_split = sem("w_split")
        w_used = sem("w_used")
        tile0_ready = sem("tile0_ready")
        tables_made, u_made = sem("tables_made"), sem("u_made")
        sqT_made, sqT_summed = sem("sqT_made"), sem("sqT_summed")
        sumT_made, mean_made = sem("sumT_made"), sem("mean_made")
        sumsq_made, rstd_made = sem("sumsq_made"), sem("rstd_made")
        h_turned, h_hi, h_split = sem("h_turned"), sem("h_hi"), sem("h_split")
        pooled, pooled_hi, pooled_split = sem("pooled"), sem("pooled_hi"), sem("pooled_split")
        tanh_made, gate_made = sem("tanh_made"), sem("gate_made")
        y0_made = sem("y0_made")
        y_turned, y_hi, y_split = sem("y_turned"), sem("y_hi"), sem("y_split")
        x1_made = sem("x1_made")
        qkv_out = [sem("q_out"), sem("k_out"), sem("v_out")]
        squared = [sem("q_squared"), sem("k_squared")]
        summed = [sem("q_summed"), sem("k_summed")]
        qk_scaled = sem("qk_scaled")
        rope_parts = [sem("q_rope_parts"), sem("k_rope_parts")]
        roped = [sem("q_roped"), sem("k_roped")]
        qk_turned = [sem("q_turned"), sem("k_turned")]
        qkT_made = [sem("qT_made"), sem("kT_made")]
        scores_ready, bias_made, exp_made = sem("scores_ready"), sem("bias_made"), sem("exp_made")
        p_turned, pT_made, o_ready, y1_made = sem("p_turned"), sem("pT_made"), sem("o_ready"), sem("y1_made")
        out_made, out_stored = sem("out_made"), sem("out_stored")
        dve_chain, pool_chain = sem("dve_chain"), sem("pool_chain")

        block = ctx.enter_context(nc.Block())

        def product_ready(eng, t, i, n):
            if t == 0:
                eng.wait_ge(tile0_ready, i + 1)
            else:
                eng.wait_ge(w_used, n + 1)

        w_in0_v = w_in0.rearrange("(k p) n -> p k n", p=P)
        w_out0_v = w_out0.rearrange("(k p) n -> p k n", p=P)
        w_in1_v = w_in1.rearrange("(k p) n -> p k n", p=P)
        w_out1_v = w_out1.rearrange("(k p) n -> p k n", p=P)

        @block.sync
        def _(sp):
            def load(slot, src, n=None):
                if n is not None:
                    sp.wait_ge(w_split, n - RING + 1)
                sp.dma_start(raw[:, slot, :].rearrange("p (k n) -> p k n", k=GK), src).then_inc(raw_landed[slot], 16)

            def load_in0(j, g, n=None):
                src = w_in0_v[:, (j % 2) * GK:(j % 2 + 1) * GK, bass.ds((j // 2) * D_INNER + g * COLS, COLS)]
                load(j, src, n)

            for b in range(KD // 2):
                sp.dma_start(xT[:, 2 * b:2 * b + 2, :], xT_in[:, 2 * b:2 * b + 2, :]).then_inc(xT_landed[b], 16)
                for i in (2 * b, 2 * b + 1):
                    n, k = i // GK, i % GK
                    sp.dma_start(raw[:, n, k * COLS:(k + 1) * COLS],
                                 w_in0_v[:, i, 0:COLS]).then_inc((*piece_landed[n], raw_landed[n])[k], 16)
            load_in0(2, 0)
            load_in0(3, 0)
            sp.dma_start(pool_mats.rearrange("p g n -> p (g n)"), pool_table).then_inc(pool_landed, 16)
            sp.dma_start(later_mats.rearrange("p g n -> p (g n)"), later_table).then_inc(pool_landed, 16)
            sp.dma_start(staged[:, 0:C_END], table).then_inc(table_landed, 16)
            sp.dma_start(staged[:, C_END:C_END + 2 * HEAD_DIM],
                         qk_gains.partition_broadcast(P)).then_inc(table_landed, 16)
            with sp.Fori(1, GROUPS) as g:
                for j in range(4):
                    load_in0(j, g, 4 * g + j)
            sp.dma_start(xs[:, :, :], x[0].rearrange("(t p) n -> p t n", p=P)).then_inc(x_landed, 16)
            for g in range(GROUPS):
                load(g, w_pool0[g].rearrange("(k p) n -> p k n", p=P), N_POOL + g)
            for h in range(2):
                for q in range(4):
                    load(q, w_out0_v[:, q * GK:(q + 1) * GK, h * COLS:(h + 1) * COLS], N_OUT0 + 4 * h + q)
            with sp.Fori(0, GROUPS) as g:
                for j in range(8):
                    src = w_in1_v[:, (j % 2) * GK:(j % 2 + 1) * GK, bass.ds((j // 2) * D_INNER + g * COLS, COLS)]
                    load(j % RING, src, N_L1 + 8 * g + j)
            for i, (h, q) in enumerate(OUT1_ORDER):
                load(i % RING, w_out1_v[:, q * GK:(q + 1) * GK, h * COLS:(h + 1) * COLS], N_OUT1 + i)
            for i in range(2 * TT):
                h, t = i // TT, i % TT
                sp.wait_ge(out_made, i + 1)
                sp.dma_start(out[0, t * P:(t + 1) * P, h * COLS:(h + 1) * COLS],
                             ysb[:, h, t, :]).then_inc(out_stored, 16)
            sp.wait_ge(out_stored, 16 * 2 * TT)

        @block.gpsimd
        def _(pool):
            chain = Chain(pool, pool_chain)
            chain.done(pool.memset(ident[:, :], 0.0))
            pool.affine_select(out=ident[:, :], in_=ident[:, :], compare_op=ALU.not_equal, fill=1.0, base=0,
                               pattern=[[-1, P]], channel_multiplier=1).then_inc(ident_made, 1)
            chain.done(pool.memset(minus_half[:, :], -0.5))
            pool.memset(ones[:, :], 1.0)
            chain.done(pool.memset(head_eps[:, :, :], HEAD_DIM * EPS))
            chain.done(pool.memset(head_root[:, :, :], HEAD_DIM ** 0.5))
            for n in range(2):
                for k in range(GK):
                    piece = slice(k * COLS, (k + 1) * COLS)
                    pool.wait_ge((*piece_landed[n], raw_landed[n])[k], 16)
                    pool.tensor_scalar(w_hi[:, n, piece], raw[:, n, piece], 1.0, 1.0, ALU.mult,
                                       ALU.mult).then_inc(piece_hi, 1)

            def row_norm():
                chain.done(pool.tensor_scalar(mean[:, :], mean[:, :], 1.0, EPS, ALU.mult, ALU.add))
                chain.done(pool.tensor_tensor(rstd[:, :], mean[:, :], minus_half[:, 0:TT], ALU.pow))
                pool.tensor_scalar(rstd_half[:, :], rstd[:, :], 0.5, 1.0, ALU.mult, ALU.mult).then_inc(rstd_made, 1)

            pool.wait_ge(raw_landed[2], 16)
            pool.tensor_scalar(w_hi[:, 2, 0:2 * COLS], raw[:, 2, 0:2 * COLS], 1.0, 1.0, ALU.mult,
                               ALU.mult).then_inc(half_hi[0], 1)
            pool.wait_ge(mean_made, 1)
            row_norm()
            chain.done(pool.memset(mask[:, :], 0.0))
            chain.done(pool.affine_select(out=mask[:, P:], in_=mask[:, P:], compare_op=ALU.is_ge, fill=MASKED,
                                          base=0, pattern=[[-1, P]], channel_multiplier=1))
            pool.wait_ge(table_landed, 2 * 16)
            half = HEAD_DIM // 2
            for i, gain in enumerate((gain_q, gain_k)):
                for t in range(TT):
                    cos = staged[:, C_COS + t * HEAD_DIM:C_COS + (t + 1) * HEAD_DIM]
                    sin = staged[:, C_SIN + t * HEAD_DIM:C_SIN + (t + 1) * HEAD_DIM]
                    pool.tensor_tensor(rope_tab[:, 2 * i, t, :], cos, gain, ALU.mult)
                    pool.tensor_tensor(rope_tab[:, 2 * i + 1, t, 0:half], sin[:, 0:half], gain[:, half:], ALU.mult)
                    last = pool.tensor_tensor(rope_tab[:, 2 * i + 1, t, half:], sin[:, half:], gain[:, 0:half],
                                              ALU.mult)
            last.then_inc(tables_made, 1)
            pool.wait_ge(sumsq_made, 2 * TT)
            chain.done(pool.tensor_tensor(mean[:, :], sumsq[:, :, 0], sumsq[:, :, 1], ALU.add))
            chain.done(pool.tensor_scalar(mean[:, :], mean[:, :], 1.0 / D_MODEL, 1.0, ALU.mult, ALU.mult))
            row_norm()

            def norm_rope(g, i, first=False):
                v = qk[i]
                pool.wait_ge(qkv_out[i], TT * (g + 1))
                pool.tensor_tensor(scratch[i], v, v, ALU.mult).then_inc(squared[i], 1)
                pool.wait_ge(summed[i], g + 1)
                chain.done(pool.tensor_tensor(qk_mean[:, i], qk_sum[:, i], head_eps[:, :, :], ALU.add))
                if i == 0 and not first:
                    pool.wait_ge(exp_made, HPG * g)
                scaled = pool.tensor_tensor(qk_rstd[:, i], qk_mean[:, i],
                                            minus_half[:, :].rearrange("p (t h) -> p t h", t=TT), ALU.pow)
                if i == 0:
                    scaled.then_inc(qk_scaled, 1)
                else:
                    chain.done(scaled)
                    chain.done(pool.tensor_tensor(qk_rstd[:, i], qk_rstd[:, i], head_root[:, :, :], ALU.mult))
                v4 = v.rearrange("p t (h d) -> p t h d", h=HPG)
                s4 = scratch[i].rearrange("p t (h d) -> p t h d", h=HPG)
                if i == 1:
                    for t in range(TT):
                        ins = pool.tensor_tensor(v4[:, t], v4[:, t],
                                                 qk_rstd[:, i, t, :].unsqueeze(2).to_broadcast([P, HPG, HEAD_DIM]),
                                                 ALU.mult)
                    chain.done(ins)
                for t in range(TT):
                    for a, b in ((0, half), (half, 0)):
                        tab = rope_tab[:, 2 * i + 1, t, a:a + half].unsqueeze(1).to_broadcast([P, HPG, half])
                        ins = pool.tensor_tensor(s4[:, t, :, a:a + half], v4[:, t, :, b:b + half], tab, ALU.mult)
                chain.done(ins)
                for t in range(TT):
                    tab = rope_tab[:, 2 * i, t, :].unsqueeze(1).to_broadcast([P, HPG, HEAD_DIM])
                    ins = pool.tensor_tensor(v4[:, t], v4[:, t], tab, ALU.mult)
                ins.then_inc(rope_parts[i], 1)

            start, per_group = chain.made, 7
            norm_rope(0, 0, first=True)
            norm_rope(0, 1, first=True)
            with pool.Fori(1, GROUPS) as g:
                chain.rebase(start + per_group * g)
                norm_rope(g, 0)
                norm_rope(g, 1)
                assert chain.made == per_group, chain.made

        @block.scalar
        def _(act):
            act.dma_start(gains[:, :], gains_in).then_inc(gains_landed, 16)
            act.wait_ge(pool_chain, 2)
            act.activation(row_sum[:, 0, 0:1], minus_half[:, 0:1], ACT.Exp)

            def weight_hi(n, slot, landed):
                act.wait_ge(raw_landed[slot], landed)
                act.wait_ge(w_used, n - RING + 1)
                act.activation(w_hi[:, slot, :], raw[:, slot, :], ACT.Copy).then_inc(hi_made, 1)

            def static_hi(n):
                weight_hi(n, n % RING, 16 * (n // RING + 1))

            def turned_hi(dst, f0, bank, turned, made, gain=None):
                act.wait_ge(turned[0], turned[1])
                if gain is None:
                    act.activation(dst[:, bass.ds(f0, 2), :].rearrange("p f s -> p (f s)"), aux[bank][:, :],
                                   ACT.Copy).then_inc(made, 1)
                    return
                for j in range(2):
                    ins = act.activation(dst[:, f0 + j, :], aux[bank][:, j * SEQ:(j + 1) * SEQ], ACT.Copy,
                                         scale=gains[:, gain + f0 + j:gain + f0 + j + 1])
                ins.then_inc(made, 1)

            def squares(t, half):
                act.activation(ysb[:, half, t], xs[:, t, half * COLS:(half + 1) * COLS], ACT.Square,
                               accum_out=sumsq[:, t, half:half + 1]).then_inc(sumsq_made, 1)

            act.wait_ge(gains_landed, 16)
            for b in range(KD // 2):
                act.wait_ge(xT_landed[b], 16)
                for k in (2 * b, 2 * b + 1):
                    ins = act.activation(hT_hi[:, k, :], xT[:, k, :], ACT.Copy, scale=gains[:, k:k + 1])
                ins.then_inc(h_hi, 1)
                act.activation(sqT[:, 2 * b * SEQ:2 * (b + 1) * SEQ],
                               xT[:, 2 * b:2 * b + 2, :].rearrange("p k s -> p (k s)"),
                               ACT.Square).then_inc(sqT_made, 1)
            act.wait_ge(raw_landed[2], 16)
            act.activation(w_hi[:, 2, 2 * COLS:], raw[:, 2, 2 * COLS:], ACT.Copy).then_inc(half_hi[1], 1)

            def mean_squares():
                act.wait_ge(sumT_made, 1)
                act.activation(mean[:, :], aux[3][:, 0:TT], ACT.Copy, scale=1.0 / D_MODEL).then_inc(mean_made, 1)

            def u_out(g):
                act.wait_ge(rstd_made, 1)
                for t in range(TT):
                    product_ready(act, t, 2 * g, 4 * g + 1)
                    act.activation(u_s[:, t, :], acc[0][t][:, :], ACT.Copy,
                                   scale=rstd[:, t:t + 1]).then_inc(u_made, 1)

            def layer0(g, first):
                if first:
                    mean_squares()
                    u_out(g)
                    act.wait_ge(raw_landed[3], 16)
                    act.activation(w_hi[:, 3, :], raw[:, 3, :], ACT.Copy).then_inc(hi_made, 1)
                    weight_hi(4, 0, 16 * 2)
                else:
                    weight_hi(4 * g + 4, 0, 16 * (g + 2))
                    u_out(g)
                weight_hi(4 * g + 5, 1, 16 * (g + 2))
                for b in range(2):
                    turned_hi(aT_hi, HPG * g + 2 * b, b, (pooled, 2 * g + b + 1), pooled_hi)
                weight_hi(4 * g + 6, 2, 16 * (g + 2))
                act.wait_ge(tables_made, 1)
                for t in range(TT):
                    product_ready(act, t, 2 * g + 1, 4 * g + 3)
                    act.activation(wide[:, t, bass.ds(g * COLS, COLS)], acc[1][t][:, :], ACT.Tanh,
                                   scale=rstd_half[:, t:t + 1]).then_inc(tanh_made, 1)
                weight_hi(4 * g + 7, 3, 16 * (g + 2))

            layer0(0, first=True)
            with act.Fori(1, GROUPS) as g:
                layer0(g, first=False)

            def y0_hi(g):
                for b in range(2):
                    turned_hi(aT_hi, HPG * g + 2 * b, 2 * (g % 2) + b, (y_turned, 2 * g + b + 1), y_hi, gain=2 * KD)

            for g in range(GROUPS):
                if g > 0:
                    static_hi(N_POOL + 3 + g)
                    y0_hi(g - 1)
            static_hi(N_OUT0 + 3)
            y0_hi(GROUPS - 1)

            def h1_hi(half):
                for t in range(TT):
                    act.wait_ge(x1_made, TT * half + t + 1)
                    if half == 0 and t == 0:
                        act.wait_ge(rstd_made, 1)
                    squares(t, half)
                for b in range(2):
                    turned_hi(hT_hi, 4 * half + 2 * b, 2 * half + b, (h_turned, 2 * half + b + 1), h_hi, gain=KD)

            for n in range(N_OUT0 + 4, N_OUT0 + 8):
                static_hi(n)
            h1_hi(0)
            for n in range(N_OUT0 + 8, N_L1 + 3):
                static_hi(n)

            def exp_scores(g, h):
                act.wait_ge(bias_made, HPG * g + h + 1)
                if h > 0:
                    act.wait_ge(p_turned, HPG * g + h)
                act.activation(probs[:, 0:P], aux[h % 2][:, 0:P], ACT.Exp, bias=exp_bias[:, h, 0:1],
                               scale=qk_rstd[:, 0, 0, h:h + 1], accum_out=row_sum[:, h, 0:1])
                act.activation(probs[:, P:3 * P], aux[h % 2][:, P:3 * P], ACT.Exp, bias=exp_bias[:, h, 1:2],
                               scale=qk_rstd[:, 0, 1, h:h + 1], accum_out=row_sum[:, h, 1:2]).then_inc(exp_made, 1)

            def probs_out(g, h):
                act.wait_ge(p_turned, HPG * g + h + 1)
                if h > 0:
                    act.wait_ge(o_ready, HPG * g + h)
                act.activation(probsT[:, :], aux[2][:, 0:3 * P], ACT.Copy).then_inc(pT_made, 1)

            def qkv_evacuate(g, which, first=False):
                if first:
                    pass
                elif which < 2:
                    act.wait_ge(qk_turned[which], 2 * g)
                else:
                    act.wait_ge(o_ready, HPG * g)
                dst = (*qk, v_s)[which]
                for t in range(TT):
                    product_ready(act, t, 14 + 4 * g + which, N_L1 + 8 * g + 2 * which + 1)
                    ins = act.activation(dst[:, t, :], acc[which % 2][t][:, :], ACT.Copy, scale=rstd[:, t:t + 1])
                    ins.then_inc(qkv_out[which], 1)

            def qkT_out(g, i):
                for b in range(2):
                    act.wait_ge(qk_turned[i], 2 * g + b + 1)
                    dst = (qT, kT)[i]
                    act.activation(dst[:, 2 * b:2 * b + 2, :].rearrange("p h s -> p (h s)"), aux[2 * i + b][:, :],
                                   ACT.Copy).then_inc(qkT_made[i], 1)

            def tanh_z(g, first):
                for t in range(TT):
                    product_ready(act, t, 17 + 4 * g, N_L1 + 8 * g + 7)
                    if not first:
                        act.wait_ge(y1_made, HPG * g)
                    act.activation(gate1[:, t, :], acc[1][t][:, :], ACT.Tanh,
                                   scale=rstd_half[:, t:t + 1]).then_inc(tanh_made, 1)

            def y1_hi(g):
                for b in range(2):
                    turned_hi(aT_hi, HPG * g + 2 * b, b, (y_turned, 8 + 2 * g + b + 1), y_hi)

            def layer1(g, attend):
                def w(j):
                    weight_hi(N_L1 + 3 + 8 * g + j, (N_L1 + 3 + j) % RING, 16 * ((N_L1 + 3 + j) // RING + 1) + 32 * g)
                w(0)
                if attend:
                    exp_scores(g - 1, 0)
                qkv_evacuate(g, 0, not attend)
                w(1)
                if attend:
                    exp_scores(g - 1, 1)
                    probs_out(g - 1, 0)
                w(2)
                if attend:
                    exp_scores(g - 1, 2)
                    probs_out(g - 1, 1)
                qkv_evacuate(g, 1, not attend)
                w(3)
                if attend:
                    exp_scores(g - 1, 3)
                    probs_out(g - 1, 2)
                w(4)
                if attend:
                    probs_out(g - 1, 3)
                w(5)
                qkv_evacuate(g, 2, not attend)
                w(6)
                qkT_out(g, 0)
                w(7)
                tanh_z(g, not attend)
                if attend:
                    y1_hi(g - 1)
                qkT_out(g, 1)

            h1_hi(1)
            act.wait_ge(rstd_made, 2)
            layer1(0, attend=False)
            with act.Fori(1, GROUPS) as g:
                layer1(g, attend=True)

            last = GROUPS - 1
            for n in range(N_OUT1 + 3, N_END):
                static_hi(n)
                j = n - N_OUT1 - 3
                if j < HPG:
                    exp_scores(last, j)
                if 1 <= j <= HPG:
                    probs_out(last, j - 1)
            y1_hi(last)

        @block.tensor
        def _(pe):
            def granule(n, slot, buf, free, src_hi, src_lo, k0, first, last, need=None, mid=None, mid_at=2,
                        halves=False):
                if first and free:
                    pe.wait_ge(*free)
                if halves:
                    pe.wait_ge(half_split, 1)
                else:
                    pe.wait_ge(w_split, n + 1)
                order = [(t, k) for t in range(TT) for k in range(GK)] if last and not mid and not need else \
                    [(t, k) for k in range(GK) for t in range(TT)]
                for i, (t, k) in enumerate(order):
                    if mid and i == mid_at * TT:
                        mid()
                    if halves and i == GK // 2 * TT:
                        pe.wait_ge(w_split, n + 1)
                    if need and t == 0:
                        need(k0 + k)
                    whi = w_hi[:, slot, k * COLS:(k + 1) * COLS]
                    wlo = w_lo[:, slot, k * COLS:(k + 1) * COLS]
                    shi = src_hi[:, k0 + k, t * P:(t + 1) * P]
                    slo = src_lo[:, k0 + k, t * P:(t + 1) * P]
                    a = acc[buf][t][:, :]
                    pe.matmul(a, shi, whi, start=first and k == 0, stop=False)
                    pe.matmul(a, shi, wlo, start=False, stop=False)
                    ins = pe.matmul(a, slo, whi, start=False, stop=last and k == GK - 1)
                    if last and k == GK - 1 and t == 0:
                        ins.then_inc(tile0_ready, 1)
                    if i == TT * GK - 1:
                        ins.then_inc(w_used, 1)

            def early_granule(n):
                for i in range(3):
                    for t, k in [(t, k) for k in range(GK) for t in range(TT)] if i < 2 else \
                            [(t, k) for t in range(TT) for k in range(GK)]:
                        if t == 0 and i == 0:
                            pe.wait_ge(h_hi, 2 * n + k // 2 + 1)
                            pe.wait_ge(piece_hi, GK * n + k + 1)
                        if t == 0 and i == 1:
                            pe.wait_ge(*((piece_split, (GK - 1) * n + k + 1) if k < GK - 1 else (w_split, n + 1)))
                        if t == 0 and i == 2:
                            pe.wait_ge(h_split, 2 * n + k // 2 + 1)
                        src, w = (hT_lo if i == 2 else hT_hi), (w_lo if i == 1 else w_hi)
                        ins = pe.matmul(acc[0][t][:, :], src[:, GK * n + k, t * P:(t + 1) * P],
                                        w[:, n, k * COLS:(k + 1) * COLS], start=(n, i, k) == (0, 0, 0),
                                        stop=(n, i, k) == (1, 2, GK - 1))
                        if n == 1 and i == 2 and k == GK - 1 and t == 0:
                            ins.then_inc(tile0_ready, 1)
                ins.then_inc(w_used, 1)

            def turn(dst_banks, src, made, tiles=range(HPG)):
                for f in tiles:
                    for t in range(TT):
                        c = (f % 2) * SEQ + t * P
                        ins = pe.transpose(aux[dst_banks[f // 2]][:, c:c + P], src[:, t, f * P:(f + 1) * P],
                                           ident[:, :])
                    if f % 2:
                        ins.then_inc(made, 1)

            pe.wait_ge(zeros_made, 1)
            for _ in range(WARM_UP):
                pe.matmul(acc[1][1][:, 0:P], zeros, zeros, start=True, stop=True)

            early_granule(0)
            early_granule(1)
            pe.wait_ge(sqT_summed, 1)
            for t in range(TT):
                ins = pe.matmul(aux[3][:, t:t + 1], sqT[:, t * P:(t + 1) * P], ones[:, :], start=True, stop=True)
            ins.then_inc(sumT_made, 1)

            def h_needed(base):
                def need(k):
                    if k % 2 == 0:
                        pe.wait_ge(h_split, base + k // 2 + 1)
                return need

            def pool_tokens(g, first):
                if first:
                    pe.wait_ge(pool_landed, 2 * 16)
                else:
                    pe.wait_ge(pooled_split, 2 * g)
                pe.wait_ge(u_made, TT * (g + 1))
                for f in range(HPG):
                    bank, c = aux[f // 2], (f % 2) * SEQ
                    pe.matmul(bank[:, c:c + BAND], u_s[:, 0, f * P:(f + 1) * P], pool_mats[:, g, :], start=True,
                              stop=False, skip_group_check=True)
                    ins = pe.matmul(bank[:, c + P:c + 2 * P], u_s[:, 1, f * P:(f + 1) * P], later_mats[:, g, :],
                                    start=False, stop=True, skip_group_check=True)
                    if f % 2:
                        ins.then_inc(pooled, 1)

            def layer0(g, first):
                for j in range(2 if first else 0, 4):
                    granule(4 * g + j, j, j // 2, None, hT_hi, hT_lo, GK * (j % 2), first=j % 2 == 0, last=j % 2 == 1,
                            halves=first and j == 2)
                    if j == 2:
                        pool_tokens(g, first)

            layer0(0, first=True)
            with pe.Fori(1, GROUPS) as g:
                layer0(g, first=False)

            def turn_y0(g):
                pe.wait_ge(y0_made, g + 1)
                if g >= 2:
                    pe.wait_ge(y_split, 2 * (g - 1))
                turn((2 * (g % 2), 2 * (g % 2) + 1), ysb[:, g % 2], y_turned)

            pe.wait_ge(ident_made, 1)
            pe.wait_ge(pooled_split, 2 * GROUPS)
            for g in range(GROUPS):
                free = (y0_made, g - 1) if g >= 2 else ((u_made, gate_made)[g], TT * GROUPS)
                granule(N_POOL + g, g, g % 2, free, aT_hi, aT_lo, HPG * g, first=True, last=True)
                if g > 0:
                    turn_y0(g - 1)

            def turn_x1(half):
                pe.wait_ge(x1_made, TT * (half + 1))
                turn((2 * half, 2 * half + 1), xs[:, :, half * COLS:(half + 1) * COLS], h_turned)

            for half in range(2):
                for q in range(4):
                    pe.wait_ge(y_split, 2 * (q + 1))
                    granule(N_OUT0 + 4 * half + q, q, half, (y0_made, 3 + half), aT_hi, aT_lo, GK * q,
                            first=q == 0, last=q == 3)
                    if (half, q) == (0, 0):
                        turn_y0(GROUPS - 1)
                    if (half, q) == (1, 0):
                        turn_x1(0)

            def scores(g, h):
                for i in range(2):
                    pe.wait_ge(qkT_made[i], 2 * (g + 1))
                if h < 2:
                    pe.wait_ge(y_split, 8 + 2 * g)
                else:
                    pe.wait_ge(exp_made, HPG * g + h - 1)
                s = aux[h % 2]
                pe.matmul(s[:, 0:P], qT[:, h, 0:P], kT[:, h, 0:P], start=True, stop=True)
                pe.matmul(s[:, P:3 * P], qT[:, h, P:SEQ], kT[:, h, :], start=True, stop=True).then_inc(scores_ready, 1)

            def turn_probs(g, h):
                pe.wait_ge(exp_made, HPG * g + h + 1)
                if h > 0:
                    pe.wait_ge(pT_made, HPG * g + h)
                for i in range(3):
                    ins = pe.transpose(aux[2][:, i * P:(i + 1) * P], probs[:, i * P:(i + 1) * P], ident[:, :])
                ins.then_inc(p_turned, 1)

            def values(g, h):
                pe.wait_ge(pT_made, HPG * g + h + 1)
                pe.wait_ge(qkv_out[2], TT * (g + 1))
                if h > 0:
                    pe.wait_ge(y1_made, HPG * g + h)
                v = [v_s[:, t, h * P:(h + 1) * P] for t in range(TT)]
                pe.matmul(aux[3][:, 0:P], probsT[:, 0:P], v[0], start=True, stop=True)
                pe.matmul(aux[3][:, P:2 * P], probsT[:, P:2 * P], v[0], start=True, stop=False)
                pe.matmul(aux[3][:, P:2 * P], probsT[:, 2 * P:3 * P], v[1], start=False,
                          stop=True).then_inc(o_ready, 1)

            def turn_qk(g, i, first):
                pe.wait_ge(roped[i], g + 1)
                if first:
                    pass
                elif i == 0:
                    pe.wait_ge(exp_made, HPG * g)
                else:
                    pe.wait_ge(y1_made, HPG * g)
                turn((2 * i, 2 * i + 1), qk[i], qk_turned[i])

            def turn_y1(g, after_q):
                pe.wait_ge(y1_made, HPG * (g + 1))
                if after_q is not None:
                    pe.wait_ge(qkT_made[0], 2 * (after_q + 1))
                turn((0, 1), y1, y_turned)

            def attend(g, j):
                if j < HPG:
                    scores(g, j)
                if 2 <= j < HPG + 2:
                    values(g, j - 2)
                if 1 <= j < HPG + 1:
                    turn_probs(g, j - 1)

            def layer1(g, first):
                for j in range(8):
                    which = j // 2
                    free = {0: (x1_made, TT) if first else (qkv_out[2], TT * g),
                            1: (x1_made, 2 * TT) if first else (gate_made, TT * (GROUPS + g)),
                            2: (qkv_out[0], TT * (g + 1)), 3: (qkv_out[1], TT * (g + 1))}[which]
                    granule(N_L1 + 8 * g + j, j % RING, which % 2, free, hT_hi, hT_lo,
                            GK * (j % 2), first=j % 2 == 0, last=j % 2 == 1,
                            need=h_needed(4) if first and j < 2 else None,
                            mid=(lambda: turn_x1(1)) if first and j == 0 else None)
                    if not first:
                        attend(g - 1, j)
                    if j == 6:
                        turn_qk(g, 0, first)
                    if j == 7:
                        if not first:
                            turn_y1(g - 1, g)
                        turn_qk(g, 1, first)

            layer1(0, first=True)
            with pe.Fori(1, GROUPS) as g:
                layer1(g, first=False)

            last = GROUPS - 1

            def turn_y1_last(b):
                pe.wait_ge(y1_made, HPG * last + 2 * b + 2)
                pe.wait_ge(exp_made, HPG * last + 3 + b)
                turn((0, 1), y1, y_turned, tiles=(2 * b, 2 * b + 1))

            def y_needed(k):
                if k % 2 == 0:
                    pe.wait_ge(y_split, 8 + k // 2 + 1)

            for j, (half, q) in enumerate(OUT1_ORDER):
                inside = {6: lambda: turn_y1_last(1), 7: None}.get(j, lambda: attend(last, j))
                granule(N_OUT1 + j, j % RING, half, ((qkv_out[2], TT * GROUPS), (gate_made, 2 * TT * GROUPS))[half],
                        aT_hi, aT_lo, GK * q, first=q == 0, last=q == 3, need=y_needed if j < 7 else None,
                        mid=inside, mid_at=0 if j == 6 else 3)
                if j == 4:
                    turn_y1_last(0)

        @block.vector
        def _(dve):
            chain = Chain(dve, dve_chain)
            dve.memset(zeros, 0.0).then_inc(zeros_made, 1)

            def weight_lo(n, slot):
                dve.wait_ge(hi_made, n - RING + 2)
                dve.tensor_tensor(w_lo[:, slot, :], raw[:, slot, :], w_hi[:, slot, :].bitcast(F32),
                                  ALU.subtract).then_inc(w_split, 1)

            def turned_lo(dst, hi_src, f0, bank, hi_sem, hi_count, made, gain=None):
                dve.wait_ge(hi_sem, hi_count)
                if gain is None:
                    dve.tensor_tensor(dst[:, bass.ds(f0, 2), :].rearrange("p f s -> p (f s)"), aux[bank][:, :],
                                      hi_src[:, bass.ds(f0, 2), :].bitcast(F32).rearrange("p f s -> p (f s)"),
                                      ALU.subtract).then_inc(made, 1)
                    return
                for j in range(2):
                    ins = dve.scalar_tensor_tensor(dst[:, f0 + j, :], aux[bank][:, j * SEQ:(j + 1) * SEQ],
                                                   gains[:, gain + f0 + j:gain + f0 + j + 1],
                                                   hi_src[:, f0 + j, :].bitcast(F32), ALU.mult, ALU.subtract)
                ins.then_inc(made, 1)

            def part_lo(n, a, b, made):
                part = slice(a * COLS, b * COLS)
                return dve.tensor_tensor(w_lo[:, n, part], raw[:, n, part], w_hi[:, n, part].bitcast(F32),
                                         ALU.subtract).then_inc(made, 1)

            def piece_lo(n, k):
                dve.wait_ge(piece_hi, GK * n + k + 1)
                part_lo(n, k, k + 1, piece_split if k < GK - 1 else w_split)

            def h0_lo(b):
                dve.wait_ge(h_hi, b + 1)
                for k in (2 * b, 2 * b + 1):
                    ins = dve.scalar_tensor_tensor(hT_lo[:, k, :], xT[:, k, :], gains[:, k:k + 1],
                                                   hT_hi[:, k, :].bitcast(F32), ALU.mult, ALU.subtract)
                ins.then_inc(h_split, 1)

            for n in range(2):
                piece_lo(n, 0)
                piece_lo(n, 1)
                h0_lo(2 * n)
                piece_lo(n, 2)
                piece_lo(n, 3)
                h0_lo(2 * n + 1)
            dve.wait_ge(sqT_made, KD // 2)
            width = KD * SEQ
            while width > SEQ:
                width //= 2
                ins = dve.tensor_tensor(sqT[:, 0:width], sqT[:, 0:width], sqT[:, width:2 * width], ALU.add)
                if width > SEQ:
                    chain.done(ins)
            ins.then_inc(sqT_summed, 1)
            dve.wait_ge(half_hi[0], 1)
            part_lo(2, 0, 2, half_split)
            dve.wait_ge(half_hi[1], 1)
            part_lo(2, 2, 4, w_split)

            def layer0(g, first):
                if first:
                    weight_lo(3, 3)
                weight_lo(4 * g + 4, 0)
                weight_lo(4 * g + 5, 1)
                for b in range(2):
                    turned_lo(aT_lo, aT_hi, HPG * g + 2 * b, b, pooled_hi, 2 * g + b + 1, pooled_split)
                for t in range(TT):
                    dve.wait_ge(tanh_made, TT * g + t + 1)
                    gate = wide[:, t, bass.ds(g * COLS, COLS)]
                    ins = dve.scalar_tensor_tensor(gate, gate, 1.0, acc[1][t][:, :], ALU.add, ALU.mult)
                    ins.then_inc(gate_made, 1)
                weight_lo(4 * g + 6, 2)
                weight_lo(4 * g + 7, 3)

            layer0(0, first=True)
            with dve.Fori(1, GROUPS) as g:
                layer0(g, first=False)

            def y0_lo(g):
                for b in range(2):
                    turned_lo(aT_lo, aT_hi, HPG * g + 2 * b, 2 * (g % 2) + b, y_hi, 2 * g + b + 1, y_split,
                              gain=2 * KD)

            dve.wait_ge(gate_made, TT * GROUPS)
            for g in range(GROUPS):
                n = N_POOL + 3 + g
                if g > 0:
                    weight_lo(n, n % RING)
                for t in range(TT):
                    product_ready(dve, t, 8 + g, N_POOL + g)
                    if g >= 2:
                        dve.wait_ge(y_turned, 2 * (g - 1))
                    ins = dve.scalar_tensor_tensor(ysb[:, g % 2, t, :], acc[g % 2][t][:, :], rstd_half[:, t:t + 1],
                                                   wide[:, t, g * COLS:(g + 1) * COLS], ALU.mult, ALU.mult)
                    if t == TT - 1:
                        ins.then_inc(y0_made, 1)
                if g > 0:
                    y0_lo(g - 1)
            weight_lo(N_OUT0 + 3, (N_OUT0 + 3) % RING)
            y0_lo(GROUPS - 1)

            def x1(half):
                dve.wait_ge(x_landed, 16)
                for t in range(TT):
                    product_ready(dve, t, 12 + half, N_OUT0 + 4 * half + 3)
                    s = xs[:, t, half * COLS:(half + 1) * COLS]
                    ins = dve.tensor_tensor(s, acc[half][t][:, :], s, ALU.add)
                    ins.then_inc(x1_made, 1)

            def h1_lo(half):
                for b in range(2):
                    turned_lo(hT_lo, hT_hi, 4 * half + 2 * b, 2 * half + b, h_hi, 4 + 2 * half + b + 1, h_split,
                              gain=KD)

            for n in range(N_OUT0 + 4, N_OUT0 + 7):
                weight_lo(n, n % RING)
            x1(0)
            weight_lo(N_OUT0 + 7, (N_OUT0 + 7) % RING)
            h1_lo(0)
            for n in range(N_OUT0 + 8, N_L1 + 3):
                weight_lo(n, n % RING)
            x1(1)

            def head_max(g, h):
                dve.wait_ge(qk_scaled, g + 1)
                dve.wait_ge(scores_ready, HPG * g + h + 1)
                dve.tensor_scalar(minus_scale[:, h, :], qk_rstd[:, 0, :, h], -1.0, 1.0, ALU.mult, ALU.mult)
                s = aux[h % 2]
                dve.tensor_tensor_reduce(s[:, 0:P], s[:, 0:P], mask[:, P:], 1.0, NO_MAX, ALU.add, ALU.max,
                                         row_max[:, h, 0:1])
                chain.done(dve.tensor_tensor_reduce(s[:, P:3 * P], s[:, P:3 * P], mask[:, :], 1.0, NO_MAX,
                                                    ALU.add, ALU.max, row_max[:, h, 1:2]))
                dve.tensor_tensor(exp_bias[:, h, :], row_max[:, h, :], minus_scale[:, h, :],
                                  ALU.mult).then_inc(bias_made, 1)

            def head_out(g, h):
                dve.wait_ge(exp_made, HPG * g + h + 1)
                chain.done(dve.reciprocal(row_inv[:, h, :], row_sum[:, h, :]))
                chain.done(dve.tensor_tensor(o_scale[:, h, :], row_inv[:, h, :], rstd_half[:, :], ALU.mult))
                dve.wait_ge(o_ready, HPG * g + h + 1)
                dve.wait_ge(y_turned, 8 + 2 * g)
                for t in range(TT):
                    ins = dve.scalar_tensor_tensor(y1[:, t, h * P:(h + 1) * P], aux[3][:, t * P:(t + 1) * P],
                                                   o_scale[:, h, t:t + 1], gate1[:, t, h * P:(h + 1) * P],
                                                   ALU.mult, ALU.mult)
                ins.then_inc(y1_made, 1)

            def sum_squares(g, i):
                dve.wait_ge(squared[i], g + 1)
                dve.tensor_reduce(qk_sum[:, i], scratch[i].rearrange("p t (h d) -> p t h d", h=HPG), AX_X,
                                  ALU.add).then_inc(summed[i], 1)

            def rope_sum(g, i):
                dve.wait_ge(rope_parts[i], g + 1)
                dve.tensor_tensor(qk[i], qk[i], scratch[i], ALU.add).then_inc(roped[i], 1)

            def gate_z(g):
                for t in range(TT):
                    dve.wait_ge(tanh_made, TT * (GROUPS + g) + t + 1)
                    ins = dve.scalar_tensor_tensor(gate1[:, t, :], gate1[:, t, :], 1.0, acc[1][t][:, :],
                                                   ALU.add, ALU.mult)
                    ins.then_inc(gate_made, 1)

            def y1_lo_bank(g, b):
                turned_lo(aT_lo, aT_hi, HPG * g + 2 * b, b, y_hi, 8 + 2 * g + b + 1, y_split)

            def y1_lo(g):
                for b in range(2):
                    y1_lo_bank(g, b)

            def layer1(g, attend):
                def w(j):
                    weight_lo(N_L1 + 3 + 8 * g + j, (N_L1 + 3 + j) % RING)
                if attend:
                    head_max(g - 1, 0)
                w(0)
                if attend:
                    head_max(g - 1, 1)
                w(1)
                if attend:
                    dve.wait_ge(gate_made, TT * (GROUPS + g))
                    head_max(g - 1, 2)
                    head_out(g - 1, 0)
                sum_squares(g, 0)
                w(2)
                if attend:
                    head_max(g - 1, 3)
                    head_out(g - 1, 1)
                w(3)
                if attend:
                    head_out(g - 1, 2)
                w(4)
                sum_squares(g, 1)
                rope_sum(g, 0)
                if attend:
                    head_out(g - 1, 3)
                w(5)
                w(6)
                rope_sum(g, 1)
                w(7)
                gate_z(g)
                if attend:
                    y1_lo(g - 1)

            h1_lo(1)
            dve.wait_ge(tables_made, 1)
            layer1(0, attend=False)
            start, per_group = chain.made, 3 * HPG
            with dve.Fori(1, GROUPS) as g:
                chain.rebase(start + per_group * (g - 1))
                layer1(g, attend=True)
                assert chain.made == per_group
            chain.rebase(start + per_group * (GROUPS - 1))

            last = GROUPS - 1
            dve.wait_ge(gate_made, TT * 2 * GROUPS)
            for j in range(6):
                if j < HPG:
                    head_max(last, j)
                if j == 5:
                    y1_lo_bank(last, 0)
                if j >= 2:
                    head_out(last, j - 2)
                n = N_OUT1 + 3 + j
                if n < N_END:
                    weight_lo(n, n % RING)
            y1_lo_bank(last, 1)
            for half in range(2):
                for t in range(TT):
                    product_ready(dve, t, 30 + half, N_OUT1 + 6 + half)
                    dve.wait_ge(y_turned, 16)
                    dve.tensor_tensor(ysb[:, half, t, :], acc[half][t][:, :], xs[:, t, half * COLS:(half + 1) * COLS],
                                      ALU.add).then_inc(out_made, 1)


_INS = ["x", "w_in0", "w_pool0", "w_out0", "w_in1", "w_out1"]


def kernel(**inputs):
    import concourse.bacc as _bacc
    from concourse import mybir as _mybir
    from concourse.bass_utils import run_bass_kernel_spmd as _run

    nc = _bacc.Bacc("TRN2", target_bir_lowering=False, num_devices=1)
    arrays, args = {}, []
    table, pool_table, later_table = constant_tables()
    xT_in = np.ascontiguousarray(np.asarray(inputs["x"])[0].reshape(SEQ, KD, P).transpose(2, 1, 0))
    gains_in = np.concatenate([np.asarray(inputs[n]) for n in ("norm0", "norm1", "pool_scale0")]).reshape(-1, P)
    gains_in = np.ascontiguousarray(gains_in.T)
    qk_gains = np.concatenate([np.asarray(inputs[n]) for n in ("q_norm1", "k_norm1")])
    laid_out = [(n, np.ascontiguousarray(inputs[n])) for n in _INS]
    laid_out += [("xT", xT_in), ("gains", gains_in), ("qk_gains", qk_gains), ("table", table),
                 ("pool_table", pool_table), ("later_table", later_table)]
    for name, a in laid_out:
        arrays[f"in_{name}_dram"] = a
        args.append(nc.dram_tensor(f"in_{name}_dram", a.shape, _mybir.dt.from_np(a.dtype), kind="ExternalInput").ap())
    args.append(nc.dram_tensor("out_0_dram", (1, SEQ, D_MODEL), F32, kind="ExternalOutput").ap())
    bass_hybrid_trunk(nc, *args)
    r = _run(nc, [arrays], core_ids=[0])
    return r.results[0]["out_0_dram"]
```
